# Optimizing a Trainium2 kernel written in Bass

```python
import math
import jax, jax.numpy as jnp
from jax import lax
import numpy as np

D_MODEL = 1024
BATCH = 1
SEQ = 1024
DEPTH = 2
DEC_BATCH = 8
DEC_SEQ = 8
PAST_LEN = 8192
PAGE_SIZE = 128

N_META = 16
N_MIXERS = 2
N_CONV_LAYERS = (DEPTH + 1) // 2
N_SSD_LAYERS = DEPTH // 2
CONV_WIDTH = 31
CONV_HIST = CONV_WIDTH - 1
D_CONV = D_MODEL
SSD_EXPAND = 2
D_INNER = SSD_EXPAND * D_MODEL
HEAD_DIM = 64
N_HEADS = D_INNER // HEAD_DIM
N_GROUPS = 8
HEADS_PER_GROUP = N_HEADS // N_GROUPS
D_STATE = 128
SSD_CONV_WIDTH = 4
SSD_CONV_HIST = SSD_CONV_WIDTH - 1
CONV_DIM = D_INNER + 2 * N_GROUPS * D_STATE
IN_PROJ_DIM = D_INNER + CONV_DIM + N_HEADS
CHUNK = 128
D_FF = -(-8 * D_MODEL // (3 * 256)) * 256
EPS = 1e-6

kernel_name = 'conformer_ssd_hybrid_step'

def rmsnorm(x, g):
    xf = x.astype(jnp.float32)
    y = xf * lax.rsqrt(jnp.mean(xf * xf, axis=-1, keepdims=True) + EPS)
    return (y * g.astype(jnp.float32)).astype(x.dtype)

def layernorm(x, g, b):
    xf = x.astype(jnp.float32)
    mu = jnp.mean(xf, axis=-1, keepdims=True)
    xc = xf - mu
    y = xc * lax.rsqrt(jnp.mean(xc * xc, axis=-1, keepdims=True) + EPS)
    return (y * g.astype(jnp.float32) + b.astype(jnp.float32)).astype(x.dtype)

def causal_dwconv(x_hist, w, b):
    c = x_hist.shape[-1]
    y = lax.conv_general_dilated(x_hist, w[:, None, :].astype(x_hist.dtype), window_strides=(1,), padding='VALID',
                                 dimension_numbers=('NWC', 'WIO', 'NWC'), feature_group_count=c)
    return y + b

def swiglu(h, wg, wu, wd):
    return (jax.nn.silu(h @ wg) * (h @ wu)) @ wd

def conformer_conv(h, hist, w_pw1, b_pw1, w_dw, b_dw, ln_g, ln_b, w_pw2, b_pw2):
    u = h @ w_pw1 + b_pw1
    g = u[..., :D_CONV] * jax.nn.sigmoid(u[..., D_CONV:])
    gh = jnp.concatenate([hist.astype(g.dtype), g], axis=1)
    new_hist = gh[:, -CONV_HIST:]
    c = causal_dwconv(gh, w_dw, b_dw)
    c = jax.nn.silu(layernorm(c, ln_g, ln_b))
    return c @ w_pw2 + b_pw2, new_hist

def ssd_scan(x, dt, A, Bm, Cm, h0, chunk):
    b, L = x.shape[:2]
    nc = L // chunk
    x = x.reshape(b, nc, chunk, N_GROUPS, HEADS_PER_GROUP, HEAD_DIM).astype(jnp.float32)
    dt = dt.reshape(b, nc, chunk, N_GROUPS, HEADS_PER_GROUP)
    Bm = Bm.reshape(b, nc, chunk, N_GROUPS, D_STATE).astype(jnp.float32)
    Cm = Cm.reshape(b, nc, chunk, N_GROUPS, D_STATE).astype(jnp.float32)
    acs = jnp.cumsum(dt * A, axis=2)
    diff = acs[:, :, :, None] - acs[:, :, None, :]
    causal = jnp.tril(jnp.ones((chunk, chunk), dtype=bool))[:, :, None, None]
    decay = jnp.exp(jnp.where(causal, diff, -jnp.inf))
    cb = jnp.einsum('bclgn,bcsgn->bclsg', Cm, Bm)
    w = cb[..., None] * decay * dt[:, :, None]
    y_diag = jnp.einsum('bclsgr,bcsgrp->bclgrp', w, x)
    decay_to_end = jnp.exp(acs[:, :, -1:] - acs)
    chunk_states = jnp.einsum('bclgn,bclgr,bclgrp->bcgrpn', Bm, decay_to_end * dt, x)
    chunk_decay = jnp.exp(acs[:, :, -1])

    def step(h, inp):
        s_c, d_c = inp
        return d_c[..., None, None] * h + s_c, h

    h_last, h_prev = lax.scan(step, h0, (jnp.swapaxes(chunk_states, 0, 1), jnp.swapaxes(chunk_decay, 0, 1)))
    h_prev = jnp.swapaxes(h_prev, 0, 1)
    y_off = jnp.einsum('bclgn,bcgrpn,bclgr->bclgrp', Cm, h_prev, jnp.exp(acs))
    y = (y_diag + y_off).reshape(b, L, N_GROUPS, HEADS_PER_GROUP, HEAD_DIM)
    return y, h_last

def ssd_mixer(h, conv_hist, ssm0, n_lead, w_in, conv_w, conv_b, dt_bias, a_log, d_skip, norm_g, w_out):
    bt, L, _ = h.shape
    zxbcdt = h @ w_in
    z = zxbcdt[..., :D_INNER]
    xbc = zxbcdt[..., D_INNER:D_INNER + CONV_DIM]
    dt_raw = zxbcdt[..., D_INNER + CONV_DIM:]
    xh = jnp.concatenate([conv_hist.astype(xbc.dtype), xbc], axis=1)
    new_conv = xh[:, -SSD_CONV_HIST:]
    xbc = jax.nn.silu(causal_dwconv(xh, conv_w, conv_b))
    xs = xbc[..., :D_INNER].reshape(bt, L, N_GROUPS, HEADS_PER_GROUP, HEAD_DIM)
    Bm = xbc[..., D_INNER:D_INNER + N_GROUPS * D_STATE].reshape(bt, L, N_GROUPS, D_STATE)
    Cm = xbc[..., D_INNER + N_GROUPS * D_STATE:].reshape(bt, L, N_GROUPS, D_STATE)
    dt = jax.nn.softplus(dt_raw.astype(jnp.float32) + dt_bias.astype(jnp.float32))
    dt = dt.reshape(bt, L, N_GROUPS, HEADS_PER_GROUP)
    A = -jnp.exp(a_log.astype(jnp.float32)).reshape(N_GROUPS, HEADS_PER_GROUP)
    state = ssm0.astype(jnp.float32).reshape(bt, N_GROUPS, HEADS_PER_GROUP, HEAD_DIM, D_STATE)
    segs = ([(0, n_lead)] if n_lead > 0 else []) + [(n_lead, L)]
    ys = []
    for s, e in segs:
        y_seg, state = ssd_scan(xs[:, s:e], dt[:, s:e], A, Bm[:, s:e], Cm[:, s:e], state, math.gcd(e - s, CHUNK))
        ys.append(y_seg)
    y = jnp.concatenate(ys, axis=1) + d_skip.astype(jnp.float32).reshape(N_GROUPS, HEADS_PER_GROUP)[:, :, None] * xs.astype(jnp.float32)
    y = y.reshape(bt, L, D_INNER)
    v = y * jax.nn.silu(z.astype(jnp.float32))
    v = v.reshape(bt, L, N_GROUPS, D_INNER // N_GROUPS)
    v = v * lax.rsqrt(jnp.mean(v * v, axis=-1, keepdims=True) + EPS)
    v = v.reshape(bt, L, D_INNER) * norm_g.astype(jnp.float32)
    out = v.astype(h.dtype) @ w_out
    return out, new_conv, state.reshape(bt, N_HEADS, HEAD_DIM, D_STATE)

def trunk(h, conv_cache, ssd_conv, ssm, n_lead, norm_mix, norm_ffn, norm_final,
          cf_w_pw1, cf_b_pw1, cf_w_dw, cf_b_dw, cf_ln_g, cf_ln_b, cf_w_pw2, cf_b_pw2,
          ssd_w_in, ssd_conv_w, ssd_conv_b, ssd_dt_bias, ssd_a_log, ssd_d, ssd_norm_g, ssd_w_out,
          ffn_w_gate, ffn_w_up, ffn_w_down):
    new_cc, new_sc, new_ss = [], [], []
    for i in range(DEPTH):
        j = i // N_MIXERS
        hn = rmsnorm(h, norm_mix[i])
        if i % N_MIXERS == 0:
            mix, cc = conformer_conv(hn, conv_cache[j], cf_w_pw1[j], cf_b_pw1[j], cf_w_dw[j], cf_b_dw[j],
                                     cf_ln_g[j], cf_ln_b[j], cf_w_pw2[j], cf_b_pw2[j])
            new_cc.append(cc)
        else:
            mix, sc, ss = ssd_mixer(hn, ssd_conv[j], ssm[j], n_lead, ssd_w_in[j], ssd_conv_w[j], ssd_conv_b[j],
                                    ssd_dt_bias[j], ssd_a_log[j], ssd_d[j], ssd_norm_g[j], ssd_w_out[j])
            new_sc.append(sc)
            new_ss.append(ss)
        h = h + mix
        h = h + swiglu(rmsnorm(h, norm_ffn[i]), ffn_w_gate[i], ffn_w_up[i], ffn_w_down[i])
    return rmsnorm(h, norm_final), jnp.stack(new_cc), jnp.stack(new_sc), jnp.stack(new_ss)

def setup_inputs(seed: int = 0) -> dict:
    key = jax.random.key(seed)
    ks = jax.random.split(key, 32)

    def nrm(k, shape, scale=1.0):
        return jax.random.normal(k, shape, jnp.float32) * scale

    NA, NB = N_CONV_LAYERS, N_SSD_LAYERS
    dt0 = jnp.exp(jax.random.uniform(ks[20], (NB, N_HEADS), jnp.float32, math.log(1e-3), math.log(1e-1)))
    return {
        'x_prompt': nrm(ks[0], (BATCH, SEQ, D_MODEL)),
        'x_sample': nrm(ks[1], (DEC_BATCH, DEC_SEQ, D_MODEL)),
        'cache_conv': nrm(ks[2], (NA, DEC_BATCH, CONV_HIST, D_CONV), 0.5),
        'state_ssd_conv': nrm(ks[3], (NB, DEC_BATCH, SSD_CONV_HIST, CONV_DIM)),
        'state_ssm': nrm(ks[4], (NB, DEC_BATCH, N_HEADS, HEAD_DIM, D_STATE), 0.1),
        'meta_tokens': nrm(ks[5], (N_META, D_MODEL)),
        'norm_mix': 1.0 + nrm(ks[6], (DEPTH, D_MODEL), 0.02),
        'norm_ffn': 1.0 + nrm(ks[7], (DEPTH, D_MODEL), 0.02),
        'norm_final': 1.0 + nrm(ks[8], (D_MODEL,), 0.02),
        'cf_w_pw1': nrm(ks[9], (NA, D_MODEL, 2 * D_CONV), D_MODEL ** -0.5),
        'cf_b_pw1': nrm(ks[10], (NA, 2 * D_CONV), 0.02),
        'cf_w_dw': nrm(ks[11], (NA, CONV_WIDTH, D_CONV), CONV_WIDTH ** -0.5),
        'cf_b_dw': nrm(ks[12], (NA, D_CONV), 0.02),
        'cf_ln_g': 1.0 + nrm(ks[13], (NA, D_CONV), 0.02),
        'cf_ln_b': nrm(ks[14], (NA, D_CONV), 0.02),
        'cf_w_pw2': nrm(ks[15], (NA, D_CONV, D_MODEL), D_CONV ** -0.5),
        'cf_b_pw2': nrm(ks[16], (NA, D_MODEL), 0.02),
        'ssd_w_in': nrm(ks[17], (NB, D_MODEL, IN_PROJ_DIM), D_MODEL ** -0.5),
        'ssd_conv_w': nrm(ks[18], (NB, SSD_CONV_WIDTH, CONV_DIM), SSD_CONV_WIDTH ** -0.5),
        'ssd_conv_b': nrm(ks[19], (NB, CONV_DIM), 0.02),
        'ssd_dt_bias': dt0 + jnp.log(-jnp.expm1(-dt0)),
        'ssd_a_log': jnp.log(jax.random.uniform(ks[21], (NB, N_HEADS), jnp.float32, 1.0, 16.0)),
        'ssd_d': 1.0 + nrm(ks[22], (NB, N_HEADS), 0.02),
        'ssd_norm_g': 1.0 + nrm(ks[23], (NB, D_INNER), 0.02),
        'ssd_w_out': nrm(ks[24], (NB, D_INNER, D_MODEL), D_INNER ** -0.5),
        'ffn_w_gate': nrm(ks[25], (DEPTH, D_MODEL, D_FF), D_MODEL ** -0.5),
        'ffn_w_up': nrm(ks[26], (DEPTH, D_MODEL, D_FF), D_MODEL ** -0.5),
        'ffn_w_down': nrm(ks[27], (DEPTH, D_FF, D_MODEL), D_FF ** -0.5),
    }

def reference(x_prompt, x_sample, cache_conv, state_ssd_conv, state_ssm, meta_tokens,
              norm_mix, norm_ffn, norm_final,
              cf_w_pw1, cf_b_pw1, cf_w_dw, cf_b_dw, cf_ln_g, cf_ln_b, cf_w_pw2, cf_b_pw2,
              ssd_w_in, ssd_conv_w, ssd_conv_b, ssd_dt_bias, ssd_a_log, ssd_d, ssd_norm_g, ssd_w_out,
              ffn_w_gate, ffn_w_up, ffn_w_down):
    weights = (norm_mix, norm_ffn, norm_final,
               cf_w_pw1, cf_b_pw1, cf_w_dw, cf_b_dw, cf_ln_g, cf_ln_b, cf_w_pw2, cf_b_pw2,
               ssd_w_in, ssd_conv_w, ssd_conv_b, ssd_dt_bias, ssd_a_log, ssd_d, ssd_norm_g, ssd_w_out,
               ffn_w_gate, ffn_w_up, ffn_w_down)
    bp = x_prompt.shape[0]
    meta = jnp.broadcast_to(meta_tokens.astype(x_prompt.dtype)[None], (bp, N_META, D_MODEL))
    hp = jnp.concatenate([meta, x_prompt], axis=1)
    cc0 = jnp.zeros((N_CONV_LAYERS, bp, CONV_HIST, D_CONV), x_prompt.dtype)
    sc0 = jnp.zeros((N_SSD_LAYERS, bp, SSD_CONV_HIST, CONV_DIM), x_prompt.dtype)
    ss0 = jnp.zeros((N_SSD_LAYERS, bp, N_HEADS, HEAD_DIM, D_STATE), jnp.float32)
    yp, cc_p, sc_p, ss_p = trunk(hp, cc0, sc0, ss0, N_META, *weights)
    y_prompt = yp[:, N_META:]
    y_sample, cc_s, sc_s, ss_s = trunk(x_sample, cache_conv, state_ssd_conv, state_ssm, 0, *weights)
    return (y_prompt, y_sample, cc_p, cc_s, sc_p, sc_s, ss_p, ss_s)


_drawn_inputs = setup_inputs


def setup_inputs(seed=0):
    import zlib

    import numpy as np

    out = dict(_drawn_inputs(seed))
    spreads = {}
    factors = {'norm_final': 2.998, 'cf_ln_b': 2.775, 'ssd_d': 8.0, 'ssd_norm_g': 4.558}
    for name, (base, spread) in spreads.items():
        noise = np.random.default_rng([zlib.crc32(name.encode()), seed]).standard_normal(out[name].shape)
        drawn = base * np.exp(spread * noise) if base else spread * noise
        out[name] = __import__('jax').numpy.asarray(drawn.astype(out[name].dtype))
    for name, factor in factors.items():
        out[name] = (out[name] * factor).astype(out[name].dtype)
    return out
```

```python
from contextlib import ExitStack

import concourse.bass as bass
from concourse import mybir

F32 = mybir.dt.float32
F32R = mybir.dt.float32r
BF16 = mybir.dt.bfloat16
ACT = mybir.ActivationFunctionType
ALU = mybir.AluOpType
ds = bass.ds

P = 128
D = 1024
KT = D // P
SEQ = 1024
META = 16
NP_ = META + SEQ
DB, DL = 8, 8
NS = DB * DL
T = NS + NP_
NC = 3
TC = T // NC
EPS = 1e-6
CW = 31
HIST = CW - 1
CT = 7
DI = 2 * D
NH, HD, NG, DS = 32, 64, 8, 128
HG = NH // NG
XBC = DI + 2 * NG * DS
SW = 4
SH = SW - 1
DFF = -(-8 * D // (3 * 256)) * 256
FP = DFF // 256
L = 104
NCH = NP_ // L
CH = 1 + NCH
NEG = -1e30
N_PAR_DMAS = 13
RA_SSD = 3 * KT
DT_NABS, DT_DTA, DT_END = 4, 25, 27

C_MIX, C_FFN, C_FIN, C_BPW1, C_BDW, C_LNG, C_LNB, C_BPW2, C_SNG = 0, 16, 32, 40, 56, 64, 72, 80, 88
C_WDW, C_CW, C_CB = 128, 384, 512
NPAR = 640

U_PW1 = 0
U_PW2 = U_PW1 + 2 * KT
U_FFN0 = U_PW2 + KT
U_SSD = U_FFN0 + 6 * FP
U_FFN1 = U_SSD + 8 * NG
U_END = U_FFN1 + 6 * FP
A_PW1 = 0
A_PW2 = A_PW1 + 6 * KT
A_FFN0 = A_PW2 + 3 * KT
A_SSD = A_FFN0 + 36 * FP
A_FFN1 = A_SSD + (18 + 24) * NG
N_PW1, N_LN, N_FFN0, N_SSD, N_FFN1, N_FIN = range(6)


def hybrid_step(nc, i, o):
    with ExitStack() as ctx:
        def sb(name, shape, dt=F32):
            return ctx.enter_context(nc.sbuf_tensor(name, shape, dt))

        def sem(name):
            return ctx.enter_context(nc.semaphore(name))

        h = sb("h", [P, KT, T])
        xhi = sb("xhi", [P, KT, T], F32R)
        xlo = sb("xlo", [P, KT, T], F32R)
        stage = sb("stage", [P, 2, 1024])
        whi = sb("whi", [P, 2, 1024], F32R)
        wlo = sb("wlo", [P, 2, 1024], F32R)
        ahi = sb("ahi", [P, 2, T], F32R)
        alo = sb("alo", [P, 2, T], F32R)
        ident = sb("ident", [P, P])
        identb = sb("identb", [P, P], BF16)
        mean_w = sb("mean_w", [P, P])
        upto = sb("upto", [P, L])
        upto_s = sb("upto_s", [NS, NS])
        same_s = sb("same_s", [NS, NS])
        of_seq = sb("of_seq", [NS, DB])
        cut = sb("cut", [P, L], BF16)
        cut_s = sb("cut_s", [NS, NS], BF16)
        params = sb("params", [P, NPAR])
        dvec = sb("dvec", [P, 2 * NG])
        eps = sb("eps", [P, 1])
        arena = sb("arena", [P, 18672])

        used = [0]

        def carve(n, start=None):
            if start is not None:
                used[0] = start
            a = arena[:, used[0]:used[0] + n]
            used[0] += n
            assert used[0] <= 18672, used[0]
            return a

        xrow = carve(9 * D, 0).rearrange("p (t d) -> p t d", t=9)
        prow = carve(NPAR).rearrange("p (t d) -> p t d", t=5)
        work = [carve(KT * TC, 0).rearrange("p (k t) -> p k t", k=KT),
                carve(KT * TC).rearrange("p (k t) -> p k t", k=KT)]
        SG = DB * (HIST + DL)
        GW = SG + HIST + NP_
        glu = [carve(GW, 0), carve(GW)]
        hist = carve(KT * DB * HIST, KT * TC).rearrange("p (k r) -> p k r", k=KT)
        tail = carve(KT * P).rearrange("p (k r) -> p k r", k=KT)
        conv = carve(KT * T, 2 * KT * TC).rearrange("p (k t) -> p k t", k=KT)
        sig = carve(NC * TC).rearrange("p (c t) -> p c t", c=NC)
        hrow = conv[:, 0:2, 0:D]
        rs = [carve(TC), carve(TC)]
        diag = [carve(CT * P).rearrange("p (t q) -> p t q", t=CT) for a in range(2)]
        trow = carve(D, 0)
        sg = carve(2 * T, 2 * KT * TC).rearrange("p (a t) -> p a t", a=2)
        actv = [carve(TC), carve(TC)]
        rs_f = [carve(TC), carve(TC)]
        RW = DB * (SH + DL) + SH + NP_
        raw = carve(RW, 0)
        xs = carve(4 * T).rearrange("p (j t) -> p j t", j=4)
        zb = carve(2 * T).rearrange("p (j t) -> p j t", j=2)
        state_p = carve(DB * DS).rearrange("p (b n) -> p b n", b=DB)
        state_n = carve(DB * P).rearrange("p (b q) -> p b q", b=DB)
        xdt = carve(256)
        xend = carve(256)
        dec = carve(HG * L)
        wts = carve(HG * L)
        btok = carve(DS)
        ytok = carve(256)
        yoff = carve(256)
        st = carve(256)
        st_d = carve(256)
        ygate = carve(2 * L)
        m0 = used[0]
        cmask = carve(DB * NS).rearrange("p (b l) -> p b l", b=DB)
        bmask = carve(DB * DS).rearrange("p (b n) -> p b n", b=DB)
        vsq = carve(2 * TC, m0).rearrange("p (j t) -> p j t", j=2)
        vf = carve(2 * TC).rearrange("p (j t) -> p j t", j=2)
        vrs = carve(TC, m0 + DB * NS + DB * DS)
        chist = carve(32 * 24).rearrange("p (m r) -> p m r", m=32)
        ctail = carve(P).rearrange("p (j r) -> p j r", j=4)
        ctrow = carve(P)
        stout = carve(256).rearrange("p (j n) -> p j n", j=2)
        in_seq = carve(DB * NS).rearrange("p (b l) -> p b l", b=DB)
        cdp = carve(2 * DB).rearrange("p (j b) -> p j b", j=2)
        V = CH * NH
        tabs = carve(5 * V).rearrange("p (a c h) -> p a c h", a=5, c=CH)
        DT, DTA, NACS, EACS, DEND = range(5)
        cend = carve(V).rearrange("p (c h) -> p c h", c=CH)
        tab = carve(5 * CH * HG).rearrange("p (a c h) -> p a c h", a=5, c=CH)
        cendg = carve(CH * HG).rearrange("p (c h) -> p c h", c=CH)
        q0 = 2 * KT * TC
        wdt = carve(KT * NH, q0).rearrange("p (k n) -> p k n", k=KT)
        dtb = carve(NH)
        alog = carve(NH)
        ev = carve(V)
        e1 = carve(V)
        e2 = carve(V)
        e3 = carve(V)
        rs_w = [carve(TC), carve(TC)]
        assert used[0] <= m0 + 2000
        crow = carve(XBC, 0)
        wdh = ahi[:, 0, 0:KT * NH].rearrange("p (k n) -> p k n", k=KT)
        wdl = alo[:, 0, 0:KT * NH].rearrange("p (k n) -> p k n", k=KT)
        orow = carve(9 * D, 2 * KT * TC).rearrange("p (t d) -> p t d", t=9)
        rs_o = [carve(TC), carve(TC)]

        bank = [ctx.enter_context(nc.psum_tensor(f"bank{b}", [P, 512], F32)) for b in range(8)]
        bc_bank, g_bank, t_bank, y_bank, m_bank = bank[3:8]

        w_landed = [sem("w_landed0"), sem("w_landed1")]
        w_hi, w_lo = sem("w_hi"), sem("w_lo")
        phase_done = sem("phase_done")
        acc_done = sem("acc_done")
        in_x, in_par, in_small, in_hist = sem("in_x"), sem("in_par"), sem("in_small"), sem("in_hist")
        passed = sem("passed")
        consts = sem("consts")
        cstep = sem("cstep")
        x_turned = sem("x_turned")
        x_kept = [sem("x_kept_even"), sem("x_kept_odd")]
        pstep, c_step, in_crow = sem("pstep"), sem("c_step"), sem("in_crow")
        n_sq, n_sum, n_root, n_inv, n_x, n_hi, n_lo = (sem(x) for x in (
            "n_sq", "n_sum", "n_root", "n_inv", "n_x", "n_hi", "n_lo"))
        mu_done, cen_done = sem("mu_done"), sem("cen_done")
        h_turned, h_kept = sem("h_turned"), sem("h_kept")
        g_ready, g_sig, g_glu, g_conv, g_step, g_tail = (sem(x) for x in (
            "g_ready", "g_sig", "g_glu", "g_conv", "g_step", "g_tail"))
        d_ready, tp_done, tp_kept = sem("d_ready"), sem("tp_done"), sem("tp_kept")
        tl_turned, tl_kept = sem("tl_turned"), sem("tl_kept")
        res_added = sem("res_added")
        f_gate, f_act, f_hi, f_lo, f_down = (sem(x) for x in (
            "f_gate", "f_act", "f_hi", "f_lo", "f_down"))
        stored = sem("stored")
        s_pre = sem("s_pre")
        dt_split, dt_mm, dt_e, dt_step, dt_acs, dt_done = (sem(x) for x in (
            "dt_split", "dt_mm", "dt_e", "dt_step", "dt_acs", "dt_done"))
        ch_turned, ch_kept = sem("ch_turned"), sem("ch_kept")
        r_ready, r_kept, r_conv, r_step, r_tail = (sem(x) for x in (
            "r_ready", "r_kept", "r_conv", "r_step", "r_tail"))
        xs_ready, z_ready = sem("xs_ready"), sem("z_ready")
        ct_turned, ct_kept, ct_out = sem("ct_turned"), sem("ct_kept"), sem("ct_out")
        tab_ready = sem("tab_ready")
        st_in, st_out, sp_out = sem("st_in"), sem("st_out"), sem("sp_out")
        st_turned, st_kept, st_scaled, st_mm, st_new = (sem(x) for x in (
            "st_turned", "st_kept", "st_scaled", "st_mm", "st_new"))
        cd_mm, cd_ready, masks = sem("cd_mm"), sem("cd_ready"), sem("masks")
        s1_done, bc_done, xdt_ready, bt_ready, e_done, w_ready = (sem(x) for x in (
            "s1_done", "bc_done", "xdt_ready", "bt_ready", "e_done", "w_ready"))
        xend_ready, s2_done, yo_done, y_ready, std_ready, st_ready = (sem(x) for x in (
            "xend_ready", "s2_done", "yo_done", "y_ready", "std_ready", "st_ready"))
        s3_done, yg_ready, v_ready = sem("s3_done"), sem("yg_ready"), sem("v_ready")
        v_sq, v_sum, v_root, v_inv, v_norm, v_hi, v_lo = (sem(x) for x in (
            "v_sq", "v_sum", "v_root", "v_inv", "v_norm", "v_hi", "v_lo"))
        so_turned, so_kept = sem("so_turned"), sem("so_kept")
        o_turned = sem("o_turned")
        o_kept = [sem("o_kept_even"), sem("o_kept_odd")]

        def wait(eng, s, n):
            if not (isinstance(n, int) and n <= 0):
                eng.wait_ge(s, n)

        def apart(eng):
            eng.nop().then_inc(passed, 1)

        def phase_end(eng, n):
            eng.drain().then_inc(phase_done, 1)
            eng.wait_ge(phase_done, 4 * n)

        def chunk(t, c):
            return t[:, :, c * TC:(c + 1) * TC]

        def keep_tokens(eng, q):
            t, k0 = q // 2, 4 * (q % 2)
            n = P if t < 8 else T - 8 * P
            eng.wait_ge(x_turned, q + 1)
            dst = h[:, k0:k0 + 4, t * P:t * P + n]
            src = bank[q % 6][:, :].rearrange("p (k t) -> p k t", k=4)[:, :, 0:n]
            (eng.tensor_copy(dst, src) if q % 2 else eng.activation(dst, src, ACT.Copy)).then_inc(x_kept[q % 2], 1)

        def keep_rows(eng, q):
            t, k0 = q // 2, 4 * (q % 2)
            n = P if t < 8 else T - 8 * P
            eng.wait_ge(o_turned, q + 1)
            dst, src = orow[0:n, t, k0 * P:k0 * P + 512], bank[q % 6][0:n, :]
            (eng.tensor_copy(dst, src) if q % 2 else eng.activation(dst, src, ACT.Copy)).then_inc(o_kept[q % 2], 1)

        def fill(c):
            return (0 if c == 0 else 2 + 22 * (c - 1) // NCH), 2 + 22 * c // NCH

        C_HALF = next(c for c in range(CH) if fill(c)[1] >= 12)

        def parts(c):
            return (c == 0, max(c * TC - NS, 0), TC - (NS if c == 0 else 0))

        block = ctx.enter_context(nc.Block())

        @block.sync
        def _(sp):
            cm = [0]

            def weights(u, slot, view, src):
                sp.wait_ge(w_lo, u + 1)
                sp.dma_start(view, src).then_inc(w_landed[slot], 16)

            def cols(u, slot, w, n0):
                weights(u, slot, stage[:, slot, :].rearrange("p (k n) -> p k n", k=KT),
                        w.rearrange("(k p) n -> p k n", p=P)[:, :, ds(n0, P)])

            def rows(u, slot, w, pair, half):
                weights(u, slot, stage[:, slot, :].rearrange("p (k n) -> p k n", k=2),
                        w.rearrange("(k p) n -> p k n", p=P)[:, ds(2 * pair, 2), half * 512:half * 512 + 512])

            xs_src, xp = i["x_sample"].rearrange("b t d -> (b t) d"), i["x_prompt"][0]
            sp.dma_start(xrow[0:NS, 0, :], xs_src).then_inc(in_x, 16)
            sp.dma_start(xrow[NS:NS + META, 0, :], i["meta_tokens"]).then_inc(in_x, 16)
            sp.dma_start(xrow[NS + META:P, 0, :], xp[0:P - NS - META, :]).then_inc(in_x, 16)
            r0 = P - NS - META
            sp.dma_start(xrow[:, 1:8, :], xp[r0:r0 + 7 * P, :].rearrange("(t p) d -> p t d", p=P)).then_inc(in_x, 16)
            rl = SEQ - r0 - 7 * P
            sp.dma_start(xrow[0:rl, 8, :], xp[r0 + 7 * P:SEQ, :]).then_inc(in_x, 16)

            def vec(tile, row, src):
                n = src.shape[0]
                sp.dma_start(prow[row:row + n, tile, :], src).then_inc(in_par, 16)
                cm[0] += 1

            sp.wait_ge(consts, 1)
            for col, name in ((C_MIX, "norm_mix"), (C_FFN, "norm_ffn")):
                vec(0, col, i[name].rearrange("l (k d) -> (l k) d", d=P))
            for col, name in ((C_BPW1, "cf_b_pw1"), (C_BDW, "cf_b_dw"), (C_LNG, "cf_ln_g"),
                              (C_LNB, "cf_ln_b"), (C_BPW2, "cf_b_pw2"), (C_SNG, "ssd_norm_g")):
                vec(0, col, i[name][0].rearrange("(k d) -> k d", d=P))
            vec(0, C_FIN, i["norm_final"].rearrange("(k d) -> k d", d=P))
            wd = i["cf_w_dw"][0].rearrange("t (k d) -> (t k) d", d=P)
            vec(1, 0, wd[0:P, :])
            vec(2, 0, wd[P:CW * KT, :])
            vec(3, 0, i["ssd_conv_w"][0].rearrange("t (k d) -> (t k) d", d=P))
            vec(4, 0, i["ssd_conv_b"][0].rearrange("(k d) -> k d", d=P))
            assert cm[0] == N_PAR_DMAS
            for half in range(2):
                sp.dma_start(dvec[half * HD:(half + 1) * HD, :],
                             i["ssd_d"][0].rearrange("(m a) -> a m", a=2)[half:half + 1, :].broadcast_to([HD, 2 * NG]),
                             allow_slow_non_contiguous=True).then_inc(in_small, 16)
            cols(0, 0, i["cf_w_pw1"][0], 0)
            cols(1, 1, i["cf_w_pw1"][0], D)
            sp.dma_start(o["cc_s"][0][:, 0:HIST - DL, :], i["cache_conv"][0][:, DL:HIST, :]).then_inc(stored, 16)
            sp.wait_ge(x_kept[0], 9)
            sp.wait_ge(x_kept[1], 9)
            sp.dma_start(hrow[0:120, 0, :], i["cache_conv"][0].rearrange("b r d -> (b r) d")[0:120, :]).then_inc(in_hist, 16)
            sp.dma_start(hrow[0:120, 1, :], i["cache_conv"][0].rearrange("b r d -> (b r) d")[120:240, :]).then_inc(in_hist, 16)
            cols(2, 0, i["cf_w_pw1"][0], P)
            cols(3, 1, i["cf_w_pw1"][0], D + P)
            with sp.Fori(1, KT // 2) as m2:
                for a in range(2):
                    cols(4 * m2 + 2 * a, 0, i["cf_w_pw1"][0], m2 * (2 * P) + a * P)
                    cols(4 * m2 + 2 * a + 1, 1, i["cf_w_pw1"][0], m2 * (2 * P) + D + a * P)
            with sp.Fori(0, KT // 2) as m2:
                for a in range(2):
                    cols(U_PW2 + 2 * m2 + a, a, i["cf_w_pw2"][0], m2 * (2 * P) + a * P)

            def ffn(layer, u0):
                g_, u_, d_ = i["ffn_w_gate"][layer], i["ffn_w_up"][layer], i["ffn_w_down"][layer]
                for j in range(2):
                    cols(u0 + j, j, g_, j * P)
                for j in range(2):
                    cols(u0 + 2 + j, j, u_, j * P)
                with sp.Fori(0, FP - 1) as f:
                    for j in range(2):
                        cols(u0 + 4 + 6 * f + j, j, g_, f * (2 * P) + (2 + j) * P)
                    for j in range(2):
                        rows(u0 + 6 + 6 * f + j, j, d_, f, j)
                    for j in range(2):
                        cols(u0 + 8 + 6 * f + j, j, u_, f * (2 * P) + (2 + j) * P)
                for j in range(2):
                    rows(u0 + 6 * FP - 2 + j, j, d_, FP - 1, j)

            ffn(0, U_FFN0)

            w_in, w_out = i["ssd_w_in"][0], i["ssd_w_out"][0]
            cols(U_SSD, 0, w_in, DI)
            cols(U_SSD + 1, 1, w_in, DI + P)
            sp.wait_ge(phase_done, 4 * 2)
            sp.dma_start(wdt, w_in.rearrange("(k p) n -> p k n", p=P)[:, :, DI + XBC:DI + XBC + NH]).then_inc(s_pre, 16)
            sp.dma_start(dtb, i["ssd_dt_bias"].broadcast_to([P, NH])).then_inc(s_pre, 16)
            sp.dma_start(alog, i["ssd_a_log"].broadcast_to([P, NH])).then_inc(s_pre, 16)
            sp.wait_ge(n_lo, NC * 4)
            sp.wait_ge(dt_split, 1)
            sp.dma_start(crow[0:24, :], i["state_ssd_conv"][0].rearrange("b r d -> (b r) d")).then_inc(in_crow, 16)

            def group(g, first, last=False):
                u = U_SSD if first else U_SSD + 8 * g - 2
                cols(u + 2, 0, w_in, g * P + 2 * DI)
                cols(u + 3, 1, w_in, g * P + 2 * DI + NG * DS)
                cols(u + 4, 0, w_in, g * 256)
                cols(u + 5, 1, w_in, g * 256 + P)
                wait(sp, st_out, 32 * g)
                sp.wait_ge(phase_done, 4 * 3)
                s_in = i["state_ssm"][0].rearrange("b (g q) p n -> g (q p) b n", g=2 * NG)
                s_o = o["ss_s"][0].rearrange("b (g q) p n -> g (q p) b n", g=2 * NG)
                sp.dma_start(state_p, s_in[ds(2 * g, 1)].rearrange("a p b n -> (a p) b n")).then_inc(st_in, 16)
                if not first:
                    rows(u + 6, 0, w_out, g - 1, 0)
                    rows(u + 7, 1, w_out, g - 1, 1)
                if last:
                    rows(u + 8, 0, w_out, g, 0)
                    rows(u + 9, 1, w_out, g, 1)
                else:
                    n = 6 if first else 8
                    cols(u + n, 0, w_in, g * 256 + DI + 256)
                    cols(u + n + 1, 1, w_in, g * 256 + DI + 256 + P)
                sp.wait_ge(ct_kept, g + 1)
                for j, c0 in enumerate((g * 256, g * 256 + P, g * P + DI, g * P + DI + NG * DS)):
                    sp.dma_start(o["sc_s"][0].rearrange("b r d -> (b r) d")[:, ds(c0, P)],
                                 ctrow[32 * j:32 * j + 24, :]).then_inc(ct_out, 16)
                    sp.dma_start(o["sc_p"][0, 0][:, ds(c0, P)], ctrow[32 * j + 24:32 * j + 27, :]).then_inc(ct_out, 16)
                for j in range(2):
                    sp.wait_ge(st_new, 4 * g + 2 * j + 2)
                    sp.dma_start(s_o[ds(2 * g + j, 1)].rearrange("a p b n -> (a p) b n"), state_p).then_inc(st_out, 16)
                    if j == 0:
                        sp.wait_ge(st_out, 32 * g + 16)
                        sp.dma_start(state_p, s_in[ds(2 * g + 1, 1)].rearrange("a p b n -> (a p) b n")).then_inc(st_in, 16)
                sp.wait_ge(so_kept, g + 1)
                sp.dma_start(o["ss_p"][0, 0].rearrange("(g j q) p n -> g (q p) j n", g=NG, j=2)[ds(g, 1)].rearrange("a p j n -> (a p) j n"),
                             stout).then_inc(sp_out, 16)

            group(0, True)
            with sp.Fori(1, NG - 1) as g:
                group(g, False)
            group(NG - 1, False, last=True)
            ffn(1, U_FFN1)

            yp, ys = o["y_p"][0], o["y_s"].rearrange("b t d -> (b t) d")
            sp.wait_ge(o_kept[0], 9)
            sp.wait_ge(o_kept[1], 9)
            sp.dma_start(ys, orow[0:NS, 0, :]).then_inc(stored, 16)
            sp.dma_start(yp[0:r0, :], orow[NS + META:P, 0, :]).then_inc(stored, 16)
            sp.dma_start(yp[r0:r0 + 7 * P, :].rearrange("(t p) d -> p t d", p=P), orow[:, 1:8, :]).then_inc(stored, 16)
            sp.dma_start(yp[r0 + 7 * P:SEQ, :], orow[0:rl, 8, :]).then_inc(stored, 16)
            sp.wait_ge(stored, 16 * (1 + 1 + DB + 4))
            sp.wait_ge(ct_out, 16 * 8 * NG)
            sp.wait_ge(st_out, 32 * NG)
            sp.wait_ge(sp_out, 16 * NG)

        @block.tensor
        def _(pe):
            def turn(out, in_, k=P):
                return pe.transpose(out, in_, ident[0:k, 0:k])

            def dense(b, slot, offs, hi, lo, c):
                cs = slice(c * TC, (c + 1) * TC)
                n = 0
                for k, w0 in enumerate(offs):
                    for w, x in ((whi, hi), (whi, lo), (wlo, hi)):
                        mm = pe.matmul(bank[b][:, 0:TC], w[:, slot, w0:w0 + P], x[:, k, cs],
                                       start=n == 0, stop=n == 3 * len(offs) - 1)
                        n += 1
                mm.then_inc(acc_done, 1)

            FULL = [k * P for k in range(KT)]

            def unit_ready(u):
                pe.wait_ge(w_lo, u + 3)

            def norm_sums(n):
                for c in range(NC):
                    q = n * NC + c
                    pe.wait_ge(n_sq, q + 1)
                    wait(pe, n_root, q - 1)
                    for k in range(KT):
                        mm = pe.matmul(bank[6 + q % 2][:, 0:TC], mean_w[:], work[c % 2][:, k, :],
                                       start=k == 0, stop=k == KT - 1)
                    mm.then_inc(n_sum, 1)

            pe.wait_ge(consts, 2)
            pe.wait_ge(in_par, 16 * N_PAR_DMAS)
            for t in range(5):
                mm = turn(bank[6 + t // 4][:, (t % 4) * P:(t % 4 + 1) * P], prow[:, t, :])
            mm.then_inc(cstep, 1)
            pe.wait_ge(in_x, 16 * 5)
            for q in range(18):
                t, k0 = q // 2, 4 * (q % 2)
                n = P if t < 8 else T - 8 * P
                wait(pe, x_kept[q % 2], q // 2 - 2)
                for k in range(4):
                    mm = turn(bank[q % 6][:, k * P:k * P + n], xrow[0:n, t, (k0 + k) * P:(k0 + k + 1) * P], n)
                mm.then_inc(x_turned, 1)
            pe.wait_ge(in_hist, 32)
            for q in range(4):
                if q == 0:
                    pe.wait_ge(x_kept[0], 9)
                    pe.wait_ge(x_kept[1], 9)
                for k in range(4):
                    mm = turn(bank[q][:, k * 120:(k + 1) * 120],
                              hrow[0:120, q % 2, (4 * (q // 2) + k) * P:(4 * (q // 2) + k + 1) * P], 120)
                mm.then_inc(h_turned, 1)
            norm_sums(N_PW1)
            pe.wait_ge(h_kept, 4)

            def pw1(m, a, first):
                for v in range(2):
                    unit_ready(U_PW1 + 2 * m + v)
                    for c in range(NC):
                        if first and v == 0:
                            pe.wait_ge(n_lo, N_PW1 * NC + c + 1)
                        if not first:
                            pe.wait_ge(g_glu, NC * m - 2 + c)
                        dense(3 * v + c, v, FULL, xhi, xlo, c)

            def taps(m, a):
                pe.wait_ge(d_ready, m + 1)
                pe.wait_ge(g_glu, NC * m + NC)
                G = glu[a]
                gs = G[:, 0:SG].rearrange("p (b r) -> p b r", b=DB)
                for c in range(NC):
                    wait(pe, tp_kept, NC * m + c - 1)
                    b = bank[6 + (a + c) % 2]
                    sample, t0, n = parts(c)
                    for q in range(CT):
                        t = CW - CT + q
                        mm = pe.matmul(b[:, TC - n:TC], diag[a][:, q, :], G[:, SG + t + t0:SG + t + t0 + n],
                                       start=q == 0, stop=q == CT - 1)
                    if sample:
                        for q in range(CT):
                            t = CW - CT + q
                            mm = pe.matmul(b[:, 0:NS], diag[a][:, q, :], gs[:, :, t:t + DL],
                                           start=q == 0, stop=q == CT - 1)
                    mm.then_inc(tp_done, 1)

            pw1(0, 0, True)
            pw1(1, 1, False)
            taps(0, 0)
            with pe.Fori(1, KT // 2) as m2:
                pw1(2 * m2, 0, False)
                taps(2 * m2 - 1, 1)
                pw1(2 * m2 + 1, 1, False)
                taps(2 * m2, 0)
            taps(KT - 1, 1)
            pe.wait_ge(g_tail, KT)
            pe.wait_ge(g_glu, NC * KT)
            for k in range(KT):
                mm = turn(bank[4 + k // 4][:, (k % 4) * P:(k % 4 + 1) * P], tail[:, k, :])
            mm.then_inc(tl_turned, 1)
            pe.wait_ge(g_conv, KT)
            for c in range(NC):
                wait(pe, cen_done, c - 1)
                for k in range(KT):
                    mm = pe.matmul(bank[c % 2][:, 0:TC], mean_w[:], conv[:, k, c * TC:(c + 1) * TC],
                                   start=k == 0, stop=k == KT - 1)
                mm.then_inc(mu_done, 1)
            norm_sums(N_LN)
            pe.wait_ge(tl_kept, 1)
            pe.wait_ge(cen_done, NC)

            def pw2(m, a, r):
                unit_ready(U_PW2 + m)
                for c in range(NC):
                    if r:
                        pe.wait_ge(n_lo, N_LN * NC + c + 1)
                    wait(pe, res_added, NC * m - 5 + c)
                    dense(3 * a + c, a, FULL, xhi, xlo, c)

            for m in range(2):
                pw2(m, m, m == 0)
            with pe.Fori(1, KT // 2) as m2:
                pw2(2 * m2, 0, False)
                pw2(2 * m2 + 1, 1, False)
            phase_end(pe, 1)

            def ffn(n, u0, layer):
                norm_sums(n)
                g0, d0, s0 = layer * 6 * FP, layer * 24 * FP, n * NC

                def gate(f, first):
                    for j in range(2):
                        unit_ready(u0 + (j if first else 6 * f - 2 + j))
                        for c in range(NC):
                            if first and j == 0:
                                pe.wait_ge(n_lo, s0 + c + 1)
                            if not first:
                                pe.wait_ge(f_act, g0 + 6 * f - 5 + 3 * j + c)
                            dense(3 * j + c, j, FULL, xhi, xlo, c)

                def up(f, first):
                    for j in range(2):
                        unit_ready(u0 + (2 + j if first else 6 * f + 2 + j))
                        for c in range(NC):
                            if first:
                                pe.wait_ge(f_gate, g0 + 3 * j + c + 1)
                            else:
                                pe.wait_ge(f_down, d0 + 24 * f - 5 + 3 * j + c)
                            dense(3 * j + c, j, FULL, xhi, xlo, c)

                def down(f, last):
                    pe.wait_ge(f_lo, g0 + 6 * f + 6)
                    for j in range(2):
                        unit_ready(u0 + (6 * FP - 2 + j if last else 6 * f + 6 + j))
                        for m in range(4):
                            for c in range(NC):
                                q = 12 * j + 3 * m + c
                                if q >= 6:
                                    pe.wait_ge(f_down, d0 + 24 * f + q - 5)
                                elif last:
                                    pe.wait_ge(f_act, g0 + 6 * f + q + 1)
                                else:
                                    pe.wait_ge(f_gate, g0 + 6 * f + 6 + q + 1)
                                dense(q % 6, j, [m * P, 512 + m * P], ahi, alo, c)

                gate(0, True)
                up(0, True)
                with pe.Fori(0, FP - 1) as f:
                    gate(f + 1, False)
                    down(f, False)
                    up(f + 1, False)
                down(FP - 1, True)

            ffn(N_FFN0, U_FFN0, 0)
            phase_end(pe, 2)

            norm_sums(N_SSD)
            pe.wait_ge(dt_split, 1)
            for c in range(CH):
                t0 = 0 if c == 0 else NS + (c - 1) * L
                if c == 0:
                    pe.wait_ge(n_lo, N_SSD * NC + NC)
                n = 0
                for k in range(KT):
                    for x, w in ((xhi, wdh), (xhi, wdl), (xlo, wdh)):
                        mm = pe.matmul(bank[0][0:L, c * NH:(c + 1) * NH], x[:, k, t0:t0 + L], w[:, k, :],
                                       start=n == 0, stop=n == 3 * KT - 1)
                        n += 1
            mm.then_inc(dt_mm, 1)
            pe.wait_ge(in_crow, 16)
            for m in range(32):
                mm = turn(bank[1 + m // 16][:, (m % 16) * 24:(m % 16 + 1) * 24], crow[0:24, m * P:(m + 1) * P], 24)
            mm.then_inc(ch_turned, 1)
            pe.wait_ge(dt_step, DT_DTA)
            pe.matmul(bank[3][0:L, NH:V], upto[0:L, :], tabs[0:L, DTA, 1:CH, :], start=True, stop=True)
            pe.matmul(bank[3][0:NS, 0:NH], upto_s[:], tabs[0:NS, DTA, 0, :], start=True, stop=True)
            pe.matmul(bank[4][:, NH:V], mean_w[0:L, :], tabs[0:L, DTA, 1:CH, :], start=True, stop=True)
            pe.matmul(bank[4][0:NS, 0:NH], same_s[:], tabs[0:NS, DTA, 0, :], start=True, stop=True).then_inc(dt_acs, 1)
            phase_end(pe, 3)

            def group(g, first, last=False):
                u = U_SSD if first else U_SSD + 8 * g - 2
                xa = A_SSD + 42 * g - (0 if first else 24)
                def proj(j, n_vsum):
                    unit_ready(u + j)
                    for c in range(NC):
                        if j == 0 and not first:
                            pe.wait_ge(res_added, RA_SSD + 24 * g - 26 + c)
                            pe.wait_ge(st_new, 4 * g)
                        elif j == 0:
                            pass
                        elif j < 4:
                            pe.wait_ge(r_kept, 12 * g + 3 * j - 2 + c)
                        elif j == 4:
                            pe.wait_ge(r_kept, 12 * g + 10 + c)
                        else:
                            pe.wait_ge(z_ready, 6 * g + c + 1)
                        dense(c, j % 2, FULL, xhi, xlo, c)
                        if j == 0 and n_vsum:
                            vsum(g - 1, c)

                for j in range(6):
                    proj(j, not first)
                    if j == 5:
                        pe.wait_ge(r_tail, 4 * g + 4)
                        wait(pe, v_root, 3 * g)
                        turn(m_bank[:, 0:P], ctail.rearrange("p j r -> p (j r)")).then_inc(ct_turned, 1)
                pe.wait_ge(tab_ready, g + 1)
                for q in range(HG):
                    mm = pe.matmul(m_bank[:, P + q * DB:P + (q + 1) * DB],
                                   tab[0:NS, DTA, 0, q:q + 1].to_broadcast([NS, P]), of_seq[:], start=True, stop=True)
                mm.then_inc(cd_mm, 1)

                def s1(c):
                    n = CH * g + c
                    t0, l = (0, NS) if c == 0 else (NS + (c - 1) * L, L)
                    if c == 0:
                        pe.wait_ge(xs_ready, 4 * g + 4)
                    else:
                        pe.wait_ge(w_ready, n)
                        pe.wait_ge(bt_ready, n)
                    for j in range(3):
                        turn(t_bank[0:L, j * P:(j + 1) * P], xs[:, j, t0:t0 + L])
                    pe.matmul(t_bank[0:l, 3 * P:3 * P + l], xs[:, 2, t0:t0 + l], xs[:, 3, t0:t0 + l],
                              start=True, stop=True).then_inc(s1_done, 1)
                    wait(pe, e_done, n)
                    if c == 0:
                        apart(pe)
                    ctm = (cut if c else cut_s)[0:l, 0:l].unsqueeze(1).to_broadcast([l, HG, l])
                    pe.matmul(bc_bank[0:l, 0:HG * l], identb[0:l, 0:l], ctm, start=True, stop=False)
                    for q in range(HG):
                        mm = pe.matmul(bc_bank[0:l, q * l:(q + 1) * l],
                                       tab[0:l, DTA, c, q:q + 1].to_broadcast([l, l]),
                                       (upto if c else upto_s)[0:l, 0:l], start=False, stop=q == HG - 1)
                    mm.then_inc(bc_done, 1)

                def s2(c):
                    n = CH * g + c
                    t0, l = (0, NS) if c == 0 else (NS + (c - 1) * L, L)
                    pe.wait_ge(w_ready, n + 1)
                    wait(pe, y_ready, n)
                    for q in range(HG):
                        pe.matmul(y_bank[0:l, q * HD:(q + 1) * HD], wts[0:l, q * l:(q + 1) * l],
                                  xdt[0:l, q * HD:(q + 1) * HD], start=True, stop=True)
                    pe.wait_ge(st_ready, n)
                    pe.wait_ge(bt_ready, n + 1)
                    pe.wait_ge(xend_ready, n + 1)
                    pe.matmul(y_bank[0:l, 256:512], xs[:, 3, t0:t0 + l], st, start=True, stop=True)
                    pe.matmul(m_bank[:, 0:256], btok[0:l, :], xend[0:l, :], start=True, stop=True).then_inc(s2_done, 1)

                def s3(c):
                    n = CH * g + c
                    l = NS if c == 0 else L
                    pe.wait_ge(y_ready, n + 1)
                    wait(pe, yg_ready, n)
                    if c == 0:
                        apart(pe)
                    for j in range(2):
                        mm = turn(g_bank[:, j * L:j * L + l], ytok[0:l, j * P:(j + 1) * P], l)
                    mm.then_inc(s3_done, 1)

                s1(0)
                pe.wait_ge(w_ready, CH * g + 1)
                pe.wait_ge(bt_ready, CH * g + 1)
                wait(pe, y_ready, CH * g)
                pe.wait_ge(cd_ready, g + 1)
                apart(pe)
                for q in range(HG):
                    pe.matmul(y_bank[0:NS, q * HD:(q + 1) * HD], wts[0:NS, q * NS:(q + 1) * NS],
                              xdt[0:NS, q * HD:(q + 1) * HD], start=True, stop=True)
                for j in range(2):
                    pe.wait_ge(st_in, 32 * g + 16 * j + 16)
                    if j == 0:
                        pe.wait_ge(z_ready, 6 * g + 6)
                    else:
                        pe.wait_ge(st_new, 4 * g + 2)
                    for b in range(DB):
                        mm = turn(bank[b // 4][:, (b % 4) * P:(b % 4 + 1) * P], state_p[:, b, :])
                    mm.then_inc(st_turned, 1)
                    pe.wait_ge(st_kept, 4 * g + 2 * j + 2)
                    pe.wait_ge(masks, 2 * g + 2)
                    for b in range(DB):
                        mm = pe.matmul(y_bank[0:NS, 256 + j * P:256 + (j + 1) * P], cmask[:, b, :], state_n[:, b, :],
                                       start=b == 0, stop=b == DB - 1)
                    if j == 1:
                        mm.then_inc(s2_done, 1)
                    pe.wait_ge(xend_ready, CH * g + 1)
                    for q in range(2):
                        pe.matmul(bank[q][:, :], xend[0:NS, j * P:(j + 1) * P],
                                  bmask[0:NS, 4 * q:4 * q + 4, :], start=True, stop=True).then_inc(st_mm, 1)
                s1(1)
                s3(0)
                for c in range(CH):
                    if c:
                        s2(c)
                    if not first:
                        for k in range(*fill(c)):
                            out_acc(g, u + 6, k, k >= 3)
                    if c + 2 < CH:
                        s1(c + 2)
                    if c:
                        s3(c)
                pe.wait_ge(st_ready, CH * g + CH)
                for j in range(2):
                    mm = turn(m_bank[:, j * P:(j + 1) * P], st[:, j * P:(j + 1) * P])
                mm.then_inc(so_turned, 1)

            def out_acc(g, u, k, behind):
                j, m, c = k // 12, k // 3 % 4, k % 3
                if k % 12 == 0:
                    unit_ready(u + j)
                if behind:
                    pe.wait_ge(res_added, RA_SSD + 24 * g - 26 + k)
                elif k == 0:
                    pe.wait_ge(v_lo, 3 * g)
                    if not isinstance(g, int) or g < NG:
                        pe.wait_ge(st_new, 4 * g + 4)
                dense(c, j, [m * P, 512 + m * P], ahi, alo, c)

            def vsum(g, c):
                pe.wait_ge(v_sq, 3 * g + c + 1)
                wait(pe, v_root, 3 * g + c)
                if c == 0:
                    pe.wait_ge(so_kept, g + 1)
                for j in range(2):
                    mm = pe.matmul(m_bank[:, 0:TC], mean_w[:], vsq[:, j, :], start=j == 0, stop=j == 1)
                mm.then_inc(v_sum, 1)

            group(0, True)
            with pe.Fori(1, NG) as g:
                group(g, False)
            for c in range(NC):
                vsum(NG - 1, c)
            for k in range(24):
                out_acc(NG, U_FFN1 - 2, k, k >= 3)
            phase_end(pe, 4)

            ffn(N_FFN1, U_FFN1, 1)
            phase_end(pe, 5)
            norm_sums(N_FIN)
            for q in range(18):
                t, k0 = q // 2, 4 * (q % 2)
                n = P if t < 8 else T - 8 * P
                pe.wait_ge(n_x, N_FIN * NC + NC)
                wait(pe, o_kept[q % 2], q // 2 - 2)
                for k in range(4):
                    mm = turn(bank[q % 6][0:n, k * P:(k + 1) * P], h[:, k0 + k, t * P:t * P + n])
                mm.then_inc(o_turned, 1)

        @block.scalar
        def _(act):
            def split(u, slot, done):
                act.wait_ge(w_landed[slot], 8 * (u - slot) + 16)
                wait(act, acc_done, done)
                act.activation(whi[:, slot, :], stage[:, slot, :], ACT.Copy).then_inc(w_hi, 1)

            def norm(n, src, affine=None):
                for c in range(NC):
                    q = n * NC + c
                    if c == 2:
                        act.wait_ge(n_lo if n != N_FIN else n_x, q - 1)
                    if n == N_LN:
                        act.wait_ge(cen_done, c + 1)
                    act.activation(work[c % 2], chunk(src, c), ACT.Square).then_inc(n_sq, 1)
                    if c:
                        rest(n, c - 1, affine)
                rest(n, NC - 1, affine)

            def root(n):
                return (rs, rs, rs_f, rs_w, rs_f, rs_o)[n]

            def rest(n, c, affine):
                q = n * NC + c
                act.wait_ge(n_sum, q + 1)
                if c == 2:
                    act.wait_ge(n_x, q - 1)
                act.activation(root(n)[c % 2], bank[6 + q % 2][:, 0:TC], ACT.Sqrt, bias=eps[:, 0:1]).then_inc(n_root, 1)
                if n == N_FIN:
                    return
                act.wait_ge(n_x, q + 1)
                if affine:
                    for k in range(KT):
                        a = act.activation(work[c % 2][:, k, :], conv[:, k, c * TC:(c + 1) * TC], ACT.Silu,
                                           bias=params[:, C_LNB + k:C_LNB + k + 1],
                                           scale=params[:, C_LNG + k:C_LNG + k + 1])
                    a.then_inc(g_step, 1)
                    act.wait_ge(g_step, c + 1)
                act.activation(chunk(xhi, c), work[c % 2], ACT.Copy).then_inc(n_hi, 1)

            split(0, 0, 0)
            split(1, 1, 0)
            act.wait_ge(cstep, 1)
            act.activation(params[:, 0:512], bank[6][:], ACT.Copy).then_inc(cstep, 1)
            act.activation(params[:, 512:640], bank[7][:, 0:P], ACT.Copy).then_inc(cstep, 1)
            for q in range(0, 18, 2):
                keep_tokens(act, q)
            act.wait_ge(consts, 2)
            act.wait_ge(x_kept[1], 9)
            act.wait_ge(x_kept[0], 9)
            norm(N_PW1, h)

            def gates(m, a, first):
                for c in range(NC):
                    act.wait_ge(acc_done, A_PW1 + 6 * m + 3 + c + 1)
                    if not first:
                        act.wait_ge(g_glu, NC * m + c - 2)
                    apart(act)
                    act.activation(sig[:, c, :], bank[3 + c][:, 0:TC], ACT.Sigmoid,
                                   bias=params[:, ds(C_BPW1 + KT + m, 1)]).then_inc(g_sig, 1)
                    if c == 0:
                        split(2 * m + 2, 0, A_PW1 + 6 * m + 3)
                split(2 * m + 3, 1, A_PW1 + 6 * m + 6)

            def tap_sums(m, a):
                for c in range(NC):
                    act.wait_ge(tp_done, NC * m + c + 1)
                    apart(act)
                    act.activation(conv[:, ds(m, 1), c * TC:(c + 1) * TC].rearrange("p a t -> p (a t)"),
                                   bank[6 + (a + c) % 2][:, 0:TC], ACT.Identity,
                                   bias=params[:, ds(C_BDW + m, 1)]).then_inc(tp_kept, 1)

            gates(0, 0, True)
            gates(1, 1, False)
            tap_sums(0, 0)
            with act.Fori(1, KT // 2) as m2:
                gates(2 * m2, 0, False)
                tap_sums(2 * m2 - 1, 1)
                gates(2 * m2 + 1, 1, False)
                tap_sums(2 * m2, 0)
            tap_sums(KT - 1, 1)
            act.wait_ge(tl_turned, 1)
            act.wait_ge(g_conv, KT)
            act.activation(trow[:, 0:512], bank[4][:], ACT.Copy)
            act.activation(trow[:, 512:1024], bank[5][:], ACT.Copy).then_inc(tl_kept, 1)
            act.wait_ge(tl_kept, 1)
            act.dma_start(o["cc_p"][0, 0], trow[0:HIST, :]).then_inc(stored, 16)
            for b in range(DB):
                act.dma_start(o["cc_s"][0, b, HIST - DL:HIST, :], trow[32 + b * DL:32 + (b + 1) * DL, :]).then_inc(stored, 16)
            act.wait_ge(stored, 16 * (2 + DB))
            norm(N_LN, conv, affine=True)
            for m in range(KT):
                split(U_PW2 + 2 + m, m % 2, A_PW2 + 3 * m + 3)
            phase_end(act, 1)

            def ffn(n, u0, layer, nxt):
                norm(n, h)
                g0 = layer * 6 * FP
                a0 = A_FFN0 if layer == 0 else A_FFN1

                def gate(f, first):
                    for j in range(2):
                        for c in range(NC):
                            act.wait_ge(acc_done, a0 + (3 * j + c + 1 if first else 36 * f - 24 + 3 * j + c + 1))
                            if not first:
                                act.wait_ge(f_act, g0 + 6 * f)
                            act.activation(sg[:, j, c * TC:(c + 1) * TC], bank[3 * j + c][:, 0:TC], ACT.Silu)\
                               .then_inc(f_gate, 1)
                        split(u0 + (2 + j if first else 6 * f + j), j, a0 + 3 * j + 3 + (0 if first else 36 * f - 24))

                def up(f, first, last=False):
                    for j in range(2):
                        for c in range(NC):
                            q = 3 * j + c
                            act.wait_ge(f_act, g0 + 6 * f + q + 1)
                            act.activation(ahi[:, j, c * TC:(c + 1) * TC], actv[q % 2], ACT.Copy).then_inc(f_hi, 1)
                        if first:
                            split(u0 + 4 + j, j, a0 + 6 + 3 * j + 3)
                        else:
                            split(u0 + 6 * f + 4 + j, j, a0 + 36 * f + 6 + 3 * j + 3)

                gate(0, True)
                up(0, True)
                with act.Fori(0, FP - 1) as f:
                    gate(f + 1, False)
                    for j in range(2):
                        split(u0 + 6 * f + 8 + j, j, a0 + 36 * f + 18 + 12 * (j + 1))
                    up(f + 1, False)
                if nxt:
                    for j in range(2):
                        split(u0 + 6 * FP + j, j, a0 + 36 * FP - 24 + 12 * (j + 1))

            ffn(N_FFN0, U_FFN0, 0, True)
            phase_end(act, 2)

            act.wait_ge(s_pre, 48)
            act.activation(wdh, wdt, ACT.Copy).then_inc(dt_e, 1)
            norm(N_SSD, h)
            act.activation(alog, alog, ACT.Exp).then_inc(dt_e, 1)
            act.wait_ge(dt_step, DT_NABS)
            act.activation(e1, e1, ACT.Exp).then_inc(dt_e, 1)
            act.wait_ge(ch_turned, 1)
            for q in range(2):
                a = act.activation(chist[:, 16 * q:16 * q + 16, :].rearrange("p m r -> p (m r)"),
                                   bank[1 + q][:, 0:16 * 24], ACT.Copy)
            a.then_inc(ch_kept, 1)
            act.wait_ge(dt_acs, 1)
            act.activation(tabs[0:L, NACS, 1:CH, :], bank[3][0:L, NH:V].rearrange("p (c h) -> p c h", h=NH), ACT.Copy, scale=-1.0)
            act.activation(tabs[0:NS, NACS, 0, :], bank[3][0:NS, 0:NH], ACT.Copy, scale=-1.0).then_inc(dt_e, 1)
            act.activation(tabs[0:L, EACS, 1:CH, :], bank[3][0:L, NH:V].rearrange("p (c h) -> p c h", h=NH), ACT.Exp)
            act.activation(tabs[0:NS, EACS, 0, :], bank[3][0:NS, 0:NH], ACT.Exp)
            act.activation(cend[:, 1:CH, :], bank[4][:, NH:V].rearrange("p (c h) -> p c h", h=NH), ACT.Exp, scale=float(D)).then_inc(dt_e, 1)
            act.wait_ge(dt_step, DT_END)
            act.activation(tabs[0:L, DEND, 1:CH, :], tabs[0:L, DEND, 1:CH, :], ACT.Exp)
            act.activation(tabs[0:NS, DEND, 0, :], tabs[0:NS, DEND, 0, :], ACT.Exp).then_inc(dt_e, 1)
            phase_end(act, 3)

            def vnorm_a(g, c):
                act.wait_ge(v_ready, CH * g + CH)
                act.activation(vsq, chunk(zb, c), ACT.Square).then_inc(v_sq, 1)

            def vnorm_b(g, c):
                act.wait_ge(v_sum, 3 * g + c + 1)
                wait(act, v_norm, 3 * g + c)
                act.activation(vrs, m_bank[:, 0:TC], ACT.Sqrt, bias=eps[:, 0:1], scale=D / 256.0).then_inc(v_root, 1)
                if c + 1 < NC:
                    vnorm_a(g, c + 1)

            def vnorm_c(g, c):
                act.wait_ge(v_norm, 3 * g + c + 1)
                act.activation(chunk(ahi, c), vf, ACT.Copy).then_inc(v_hi, 1)

            def group(g, first):
                u = U_SSD if first else U_SSD + 8 * g - 2
                xa = A_SSD if first else A_SSD + 42 * g - 24
                for j in range(4):
                    for c in range(NC):
                        if j == 0 and not first:
                            if c == 0:
                                vnorm_a(g - 1, 0)
                            vnorm_b(g - 1, c)
                        act.wait_ge(acc_done, xa + 3 * j + c + 1)
                        if c == 0:
                            act.wait_ge(r_ready, 4 * g + j + 1)
                        sample, t0, n = parts(c)
                        if sample:
                            act.activation(raw[:, 0:DB * (SH + DL)].rearrange("p (b r) -> p b r", b=DB)[:, :, SH:SH + DL],
                                           bank[c][:, 0:NS].rearrange("p (b r) -> p b r", b=DB), ACT.Copy)
                        r1 = DB * (SH + DL) + SH + t0
                        act.activation(raw[:, r1:r1 + n], bank[c][:, TC - n:TC], ACT.Copy).then_inc(r_kept, 1)
                        if j == 0 and not first:
                            vnorm_c(g - 1, c)
                    split(u + j + 2, j % 2, xa + 3 * j + 3)
                    if j > 0:
                        silu(g, j - 1)
                silu(g, 3)
                for j in range(2):
                    for c in range(NC):
                        act.wait_ge(acc_done, xa + 12 + 3 * j + c + 1)
                        act.activation(zb[:, j, c * TC:(c + 1) * TC], bank[c][:, 0:TC], ACT.Silu).then_inc(z_ready, 1)
                    split(u + j + 6, j, xa + 12 + 3 * j + 3)
                act.wait_ge(ct_turned, g + 1)
                act.wait_ge(cd_mm, g + 1)
                wait(act, ct_out, 128 * g)
                act.activation(ctrow, m_bank[:, 0:P], ACT.Copy).then_inc(ct_kept, 1)
                for a in range(2):
                    ps = slice(a * HD, (a + 1) * HD)
                    v = act.activation(cdp[ps], m_bank[ps, P:P + HG * DB].rearrange("p (j a b) -> p j a b", j=2, a=2)[:, :, a, :],
                                       ACT.Exp)
                v.then_inc(cd_ready, 1)
                chunk_a(g, 0)
                for j in range(2):
                    act.wait_ge(st_turned, 2 * g + j + 1)
                    for q in range(2):
                        act.activation(state_n[:, 4 * q:4 * q + 4, :].rearrange("p b q -> p (b q)"), bank[q][:], ACT.Copy)\
                           .then_inc(st_kept, 1)
                for c in range(1, CH):
                    chunk_a(g, c)
                    if not first and c == C_HALF + 1:
                        split(u + 8, 0, xa + 30)
                if not first:
                    split(u + 9, 1, xa + 42)
                act.wait_ge(so_turned, g + 1)
                wait(act, sp_out, 16 * g)
                act.activation(stout.rearrange("p j n -> p (j n)"), m_bank[:, 0:256], ACT.Copy).then_inc(so_kept, 1)

            def silu(g, j):
                act.wait_ge(r_conv, 4 * g + j + 1)
                act.activation(xs[:, j, :], xs[:, j, :], ACT.Silu).then_inc(xs_ready, 1)

            def chunk_a(g, c):
                n = CH * g + c
                l = NS if c == 0 else L
                act.wait_ge(bc_done, n + 1)
                wait(act, w_ready, n)
                for q in range(HG):
                    a = act.activation(dec[0:l, q * l:(q + 1) * l], bc_bank[0:l, q * l:(q + 1) * l], ACT.Exp,
                                       bias=tab[0:l, NACS, c, q:q + 1])
                a.then_inc(e_done, 1)
                act.wait_ge(s1_done, n + 1)
                wait(act, s2_done, n)
                if c == 1:
                    act.wait_ge(masks, 2 * g + 2)
                    act.wait_ge(st_mm, 4 * g + 4)
                act.activation(btok[0:l, :], t_bank[0:l, 256:384], ACT.Copy).then_inc(bt_ready, 1)

            group(0, True)
            with act.Fori(1, NG) as g:
                group(g, False)
            vnorm_a(NG - 1, 0)
            for c in range(NC):
                vnorm_b(NG - 1, c)
                vnorm_c(NG - 1, c)
            for j in range(2):
                split(U_FFN1 + j, j, A_FFN1 - 24 + 12 * (j + 1))
            phase_end(act, 4)
            ffn(N_FFN1, U_FFN1, 1, False)
            phase_end(act, 5)
            norm(N_FIN, h)
            for q in range(0, 18, 2):
                keep_rows(act, q)

        @block.vector
        def _(dve):
            def norm(n, src, gain):
                for c in range(NC):
                    q = n * NC + c
                    r = (rs, rs, rs_f, rs_w, rs_f, rs_o)[n][c % 2]
                    dve.wait_ge(n_root, q + 1)
                    dve.reciprocal(r, r).then_inc(n_inv, 1)
                    dve.wait_ge(n_inv, q + 1)
                    for k in range(KT):
                        dst = h[:, k, c * TC:(c + 1) * TC] if n == N_FIN else work[c % 2][:, k, :]
                        v = dve.scalar_tensor_tensor(dst, src[:, k, c * TC:(c + 1) * TC],
                                                     params[:, gain + k:gain + k + 1], r, ALU.mult, ALU.mult)
                    v.then_inc(n_x, 1)

            for q in range(1, 18, 2):
                keep_tokens(dve, q)
            dve.wait_ge(cstep, 3)
            dve.wait_ge(in_small, 32)
            norm(N_PW1, h, C_MIX)
            for q in range(4):
                dve.wait_ge(h_turned, q + 1)
                if q == 0:
                    dve.wait_ge(n_lo, NC)
                dve.tensor_copy(hist[:, 4 * (q // 2):4 * (q // 2) + 4, 120 * (q % 2):120 * (q % 2) + 120],
                                bank[q][:, 0:480].rearrange("p (k r) -> p k r", k=4)).then_inc(h_kept, 1)

            def glu_tile(m, a, first):
                G = glu[a]
                gs = G[:, 0:SG].rearrange("p (b r) -> p b r", b=DB)
                for c in range(NC):
                    dve.wait_ge(g_sig, NC * m + c + 1)
                    if c == 0:
                        dve.wait_ge(g_ready, m + 1)
                    sample, t0, n = parts(c)
                    b_a = params[:, ds(C_BPW1 + m, 1)]
                    s = sig[:, c, :]
                    if sample:
                        dve.scalar_tensor_tensor(gs[:, :, HIST:HIST + DL], bank[c][:, 0:NS].rearrange("p (b r) -> p b r", b=DB),
                                                 b_a, s[:, 0:NS].rearrange("p (b r) -> p b r", b=DB), ALU.add, ALU.mult)
                    dve.scalar_tensor_tensor(G[:, SG + HIST + t0:SG + HIST + t0 + n], bank[c][:, TC - n:TC],
                                             b_a, s[:, TC - n:TC], ALU.add, ALU.mult).then_inc(g_glu, 1)
                dve.wait_ge(g_glu, NC * m + NC)

            def conv_tile(m, a):
                G = glu[a]
                gs = G[:, 0:SG].rearrange("p (b r) -> p b r", b=DB)
                dve.wait_ge(tp_kept, NC * m + NC)
                cs = conv[:, ds(m, 1), 0:NS].rearrange("p a (b r) -> p (a b) r", b=DB)
                cp = conv[:, ds(m, 1), NS:T].rearrange("p a t -> p (a t)")
                base = 2 * (CW - CT) * m
                for t in range(CW - CT):
                    w = params[:, ds(C_WDW + t * KT + m, 1)]
                    if t:
                        dve.wait_ge(c_step, base + 2 * t - 1)
                    dve.scalar_tensor_tensor(cp, G[:, SG + t:SG + t + NP_], w, cp, ALU.mult, ALU.add).then_inc(c_step, 1)
                    if t:
                        dve.wait_ge(c_step, base + 2 * t)
                    dve.scalar_tensor_tensor(cs, gs[:, :, t:t + DL], w, cs, ALU.mult, ALU.add).then_inc(c_step, 1)
                dve.wait_ge(c_step, base + 2 * (CW - CT))
                dve.nop().then_inc(g_conv, 1)

            glu_tile(0, 0, True)
            glu_tile(1, 1, False)
            conv_tile(0, 0)
            with dve.Fori(1, KT // 2) as m2:
                glu_tile(2 * m2, 0, False)
                conv_tile(2 * m2 - 1, 1)
                glu_tile(2 * m2 + 1, 1, False)
                conv_tile(2 * m2, 0)
            conv_tile(KT - 1, 1)
            for c in range(NC):
                dve.wait_ge(mu_done, c + 1)
                dve.tensor_tensor(chunk(conv, c), chunk(conv, c),
                                  bank[c % 2][:, 0:TC].unsqueeze(1).to_broadcast([P, KT, TC]), ALU.subtract)\
                   .then_inc(cen_done, 1)
            for c in range(NC):
                q = N_LN * NC + c
                dve.wait_ge(n_root, q + 1)
                dve.reciprocal(rs[c % 2], rs[c % 2]).then_inc(n_inv, 1)
                dve.wait_ge(n_inv, q + 1)
                dve.wait_ge(n_sum, q + 1)
                dve.tensor_tensor(chunk(conv, c), chunk(conv, c),
                                  rs[c % 2].unsqueeze(1).to_broadcast([P, KT, TC]), ALU.mult).then_inc(n_x, 1)

            def res(m, a):
                for c in range(NC):
                    dve.wait_ge(acc_done, A_PW2 + NC * m + c + 1)
                    hm = h[:, ds(m, 1), c * TC:(c + 1) * TC].rearrange("p a t -> p (a t)")
                    dve.scalar_tensor_tensor(hm, bank[3 * a + c][:, 0:TC], params[:, ds(C_BPW2 + m, 1)], hm,
                                             ALU.add, ALU.add).then_inc(res_added, 1)

            with dve.Fori(0, KT // 2) as m2:
                res(2 * m2, 0)
                res(2 * m2 + 1, 1)
            phase_end(dve, 1)

            def ffn(n, layer):
                norm(n, h, C_FFN + KT * layer)
                g0 = layer * 6 * FP
                a0 = A_FFN0 if layer == 0 else A_FFN1

                def up(f, first):
                    def lo(q):
                        j, c = q // 3, q % 3
                        dve.wait_ge(f_hi, g0 + 6 * f + q + 1)
                        cs = slice(c * TC, (c + 1) * TC)
                        dve.tensor_tensor(alo[:, j, cs], actv[q % 2], ahi[:, j, cs].bitcast(F32), ALU.subtract)\
                           .then_inc(f_lo, 1)

                    for q in range(6):
                        j, c = q // 3, q % 3
                        dve.wait_ge(acc_done, a0 + (6 + q + 1 if first else 36 * f + 6 + q + 1))
                        dve.wait_ge(f_gate, g0 + 6 * f + q + 1)
                        wait(dve, f_lo, g0 + 6 * f + q - 1)
                        dve.tensor_tensor(actv[q % 2], sg[:, j, c * TC:(c + 1) * TC], bank[q][:, 0:TC], ALU.mult)\
                           .then_inc(f_act, 1)
                        if q:
                            lo(q - 1)
                    lo(5)

                def down(f, last):
                    for q in range(24):
                        j, m, c = q // 12, q // 3 % 4, q % 3
                        dve.wait_ge(acc_done, a0 + (36 * FP - 24 if last else 36 * f + 18) + q + 1)
                        hm = h[:, 4 * j + m, c * TC:(c + 1) * TC]
                        dve.tensor_tensor(hm, hm, bank[q % 6][:, 0:TC], ALU.add).then_inc(f_down, 1)

                up(0, True)
                with dve.Fori(0, FP - 1) as f:
                    down(f, False)
                    up(f + 1, False)
                down(FP - 1, True)

            ffn(N_FFN0, 0)
            phase_end(dve, 2)

            dve.wait_ge(s_pre, 48)
            dve.wait_ge(dt_e, 1)
            dve.tensor_tensor(wdl, wdt, wdh.bitcast(F32), ALU.subtract).then_inc(dt_split, 1)
            norm(N_SSD, h, C_MIX + KT)
            nstep = [0]
            dve.memset(tabs, 0.0).then_inc(dt_step, 1)
            nstep[0] += 1
            dve.wait_ge(dt_step, 1)

            def step(ins):
                nstep[0] += 1
                ins.then_inc(dt_step, 1)
                dve.wait_ge(dt_step, nstep[0])

            dve.wait_ge(dt_mm, 1)
            hb = [L, CH, NH]
            e3c = lambda t: t[0:L].rearrange("p (c h) -> p c h", h=NH)
            step(dve.tensor_tensor(e3c(ev), bank[0][0:L, 0:V].rearrange("p (c h) -> p c h", h=NH),
                                   dtb[0:L].unsqueeze(1).to_broadcast(hb), ALU.add))
            step(dve.tensor_scalar(e1[0:L], ev[0:L], -1.0, None, ALU.mult))
            step(dve.tensor_tensor(e1[0:L], e1[0:L], ev[0:L], ALU.min))
            assert nstep[0] == DT_NABS
            dve.wait_ge(dt_e, 3)
            step(dve.tensor_scalar(e2[0:L], e1[0:L], 2.0, None, ALU.add))
            step(dve.reciprocal(e2[0:L], e2[0:L]))
            step(dve.tensor_tensor(e1[0:L], e1[0:L], e2[0:L], ALU.mult))
            step(dve.tensor_tensor(e2[0:L], e1[0:L], e1[0:L], ALU.mult))
            step(dve.tensor_scalar(e3[0:L], e2[0:L], 2.0 / 15, 2.0 / 13, ALU.mult, ALU.add))
            for k in (11, 9, 7, 5, 3, 1):
                step(dve.tensor_tensor(e3[0:L], e3[0:L], e2[0:L], ALU.mult))
                step(dve.tensor_scalar(e3[0:L], e3[0:L], 2.0 / k, None, ALU.add))
            step(dve.tensor_tensor(e3[0:L], e3[0:L], e1[0:L], ALU.mult))
            flat = lambda a: tabs[0:L, a, :, :].rearrange("p c h -> p (c h)")
            step(dve.scalar_tensor_tensor(flat(DT), ev[0:L], 0.0, e3[0:L], ALU.max, ALU.add))
            step(dve.tensor_scalar(alog, alog, -1.0, None, ALU.mult))
            step(dve.tensor_tensor(tabs[0:L, DTA, :, :], tabs[0:L, DT, :, :],
                                   alog[0:L].unsqueeze(1).to_broadcast(hb), ALU.mult))
            assert nstep[0] == DT_DTA, nstep[0]
            dve.wait_ge(dt_acs, 1)
            dve.wait_ge(dt_e, 5)
            step(dve.scalar_tensor_tensor(tabs[0:L, DEND, 1:CH, :].rearrange("p c h -> p (c h)"),
                                          bank[4][0:L, NH:V], float(D),
                                          tabs[0:L, NACS, 1:CH, :].rearrange("p c h -> p (c h)"), ALU.mult, ALU.add))
            step(dve.tensor_tensor(tabs[0:NS, DEND, 0, :], bank[4][0:NS, 0:NH], tabs[0:NS, NACS, 0, :], ALU.add))
            assert nstep[0] == DT_END
            phase_end(dve, 3)

            def vnorm(g, c):
                dve.wait_ge(v_root, 3 * g + c + 1)
                dve.reciprocal(vrs, vrs).then_inc(v_inv, 1)
                dve.wait_ge(v_inv, 3 * g + c + 1)
                wait(dve, v_lo, 3 * g + c)
                for j in range(2):
                    v = dve.scalar_tensor_tensor(vf[:, j, :], zb[:, j, c * TC:(c + 1) * TC],
                                                 params[:, ds(C_SNG + 2 * g + j, 1)], vrs, ALU.mult, ALU.mult)
                v.then_inc(v_norm, 1)
                dve.wait_ge(v_hi, 3 * g + c + 1)
                dve.tensor_tensor(chunk(alo, c), vf, chunk(ahi, c).bitcast(F32), ALU.subtract).then_inc(v_lo, 1)

            def group(g, first):
                if not first:
                    dve.wait_ge(e_done, CH * g)
                    dve.wait_ge(s2_done, CH * g)
                    dve.wait_ge(s3_done, CH * g)
                    dve.wait_ge(v_ready, CH * g)
                    dve.wait_ge(std_ready, CH * g)
                    dve.wait_ge(xend_ready, CH * g)
                dve.tensor_copy(tab[0:L, :, 1:CH, :], tabs[0:L, :, 1:CH, ds(HG * g, HG)])
                dve.tensor_copy(tab[0:NS, :, 0, :], tabs[0:NS, :, 0, ds(HG * g, HG)])
                dve.tensor_copy(cendg[:, 1:CH, :], cend[:, 1:CH, ds(HG * g, HG)]).then_inc(tab_ready, 1)
                if not first:
                    for c in range(NC):
                        vnorm(g - 1, c)
                for j in range(4):
                    dve.wait_ge(r_kept, 12 * g + 3 * j + 3)
                    if j == 0:
                        wait(dve, s3_done, CH * g)
                    tile = (2 * g, 2 * g + 1, 2 * NG + g, 3 * NG + g)[j]
                    rsm = raw[:, 0:DB * (SH + DL)].rearrange("p (b r) -> p b r", b=DB)
                    rp = raw[:, DB * (SH + DL):RW]
                    os_ = xs[:, j, 0:NS].rearrange("p (b r) -> p b r", b=DB)
                    op = xs[:, j, NS:T]
                    for t in range(SW):
                        w = params[:, ds(C_CW + 32 * t + tile, 1)]
                        base = 8 * (4 * g + j)
                        if t == 0:
                            b = params[:, ds(C_CB + tile, 1)]
                            dve.tensor_scalar(op, rp[:, 0:NP_], w, b, ALU.mult, ALU.add).then_inc(r_step, 1)
                            dve.tensor_scalar(os_, rsm[:, :, 0:DL], w, b, ALU.mult, ALU.add).then_inc(r_step, 1)
                        else:
                            dve.wait_ge(r_step, base + 2 * t - 1)
                            dve.scalar_tensor_tensor(op, rp[:, t:t + NP_], w, op, ALU.mult, ALU.add).then_inc(r_step, 1)
                            dve.wait_ge(r_step, base + 2 * t)
                            dve.scalar_tensor_tensor(os_, rsm[:, :, t:t + DL], w, os_, ALU.mult, ALU.add).then_inc(r_step, 1)
                    dve.wait_ge(r_step, base + 8)
                    dve.nop().then_inc(r_conv, 1)
                chunk_in(g, 0)
                for j in range(2):
                    for q in range(2):
                        dve.wait_ge(st_mm, 4 * g + 2 * j + q + 1)
                        dve.wait_ge(st_scaled, 2 * g + j + 1)
                        sl = state_p[:, 4 * q:4 * q + 4, :].rearrange("p b n -> p (b n)")
                        dve.tensor_tensor(sl, sl, bank[q][:], ALU.add).then_inc(st_new, 1)
                chunk_y(g, 0)
                wait(dve, so_turned, g)
                dve.memset(st, 0.0).then_inc(st_ready, 1)
                chunk_in(g, 1)
                for c in range(CH):
                    if c:
                        chunk_st(g, c)
                        if c + 1 < CH:
                            chunk_in(g, c + 1)
                        chunk_y(g, c)
                    else:
                        gate(g, 0)
                    if not first:
                        for k in range(*fill(c)):
                            out_res(g, k)
                    if c:
                        gate(g, c)

            def out_res(g, k):
                j, m, c = k // 12, k // 3 % 4, k % 3
                dve.wait_ge(acc_done, A_SSD + 42 * g - 24 + (18 if not isinstance(g, int) or g < NG else 0) + k + 1)
                hm = h[:, 4 * j + m, c * TC:(c + 1) * TC]
                dve.tensor_tensor(hm, hm, bank[c][:, 0:TC], ALU.add).then_inc(res_added, 1)

            def chunk_in(g, c):
                n = CH * g + c
                l = NS if c == 0 else L
                dve.wait_ge(s1_done, n + 1)
                wait(dve, s2_done, n)
                wait(dve, xend_ready, n)
                dve.wait_ge(bt_ready, n + 1)
                if c == 1:
                    dve.wait_ge(st_mm, 4 * g + 4)
                dve.tensor_tensor(xdt[0:l].rearrange("p (q e) -> p q e", q=HG),
                                  t_bank[0:l, 0:256].rearrange("p (q e) -> p q e", q=HG),
                                  tab[0:l, DT, c, :].unsqueeze(2).to_broadcast([l, HG, HD]), ALU.mult).then_inc(xdt_ready, 1)
                dve.wait_ge(e_done, n + 1)
                dve.tensor_tensor(wts[0:l, 0:HG * l].rearrange("p (q e) -> p q e", q=HG),
                                  dec[0:l, 0:HG * l].rearrange("p (q e) -> p q e", q=HG),
                                  t_bank[0:l, 384:384 + l].unsqueeze(1).to_broadcast([l, HG, l]), ALU.mult)\
                   .then_inc(w_ready, 1)

            def chunk_st(g, c):
                n = CH * g + c
                dve.wait_ge(s2_done, n + 1)
                dve.wait_ge(std_ready, n + 1)
                dve.tensor_tensor(st, st_d, m_bank[:, 0:256], ALU.add).then_inc(st_ready, 1)

            def chunk_y(g, c):
                n = CH * g + c
                l = NS if c == 0 else L
                dve.wait_ge(s2_done, n + 1)
                wait(dve, s3_done, n)
                dve.tensor_tensor(yoff[0:l].rearrange("p (q e) -> p q e", q=HG),
                                  y_bank[0:l, 256:512].rearrange("p (q e) -> p q e", q=HG),
                                  tab[0:l, EACS, c, :].unsqueeze(2).to_broadcast([l, HG, HD]), ALU.mult).then_inc(yo_done, 1)
                dve.wait_ge(yo_done, n + 1)
                dve.tensor_tensor(ytok[0:l], yoff[0:l], y_bank[0:l, 0:256], ALU.add).then_inc(y_ready, 1)

            def gate(g, c):
                n = CH * g + c
                t0, l = (0, NS) if c == 0 else (NS + (c - 1) * L, L)
                dve.wait_ge(s3_done, n + 1)
                wait(dve, v_ready, n)
                for j in range(2):
                    v = dve.scalar_tensor_tensor(ygate[:, j * L:j * L + l], xs[:, j, t0:t0 + l],
                                                 dvec[:, ds(2 * g + j, 1)], g_bank[:, j * L:j * L + l],
                                                 ALU.mult, ALU.add)
                v.then_inc(yg_ready, 1)

            group(0, True)
            with dve.Fori(1, NG) as g:
                group(g, False)
            for c in range(NC):
                vnorm(NG - 1, c)
            for k in range(24):
                out_res(NG, k)
            phase_end(dve, 4)
            ffn(N_FFN1, 1)
            phase_end(dve, 5)
            norm(N_FIN, h, C_FIN)
            for q in range(1, 18, 2):
                keep_rows(dve, q)

        @block.gpsimd
        def _(pool):
            pool.nop().then_inc(w_lo, 2)
            n_c = [0]

            def step(ins):
                ins.then_inc(pstep, 1)
                n_c[0] += 1
                pool.wait_ge(pstep, n_c[0])

            pool.memset(prow, 0.0).then_inc(consts, 1)
            pool.memset(eps[:], EPS)
            pool.memset(mean_w[:], 1.0 / D)
            step(pool.memset(ident[:], 0.0))
            step(pool.affine_select(out=ident[:], in_=ident[:], compare_op=ALU.not_equal, fill=1.0, base=0,
                                    pattern=[[-1, P]], channel_multiplier=1))
            step(pool.tensor_copy(identb[:], ident[:]))
            step(pool.memset(upto[:], 1.0))
            step(pool.affine_select(out=upto[:], in_=upto[:], compare_op=ALU.is_ge, fill=0.0, base=0,
                                    pattern=[[1, L]], channel_multiplier=-1))
            step(pool.memset(cut[:], 0.0))
            step(pool.affine_select(out=cut[:], in_=cut[:], compare_op=ALU.is_ge, fill=NEG, base=0,
                                    pattern=[[1, L]], channel_multiplier=-1))
            v = same_s[:].rearrange("p (b r) -> p b r", b=DB)
            step(pool.memset(same_s[:], 1.0))
            step(pool.affine_select(out=v, in_=v, compare_op=ALU.is_ge, fill=0.0, base=0,
                                    pattern=[[-DL, DB], [0, DL]], channel_multiplier=1))
            step(pool.affine_select(out=v, in_=v, compare_op=ALU.is_ge, fill=0.0, base=DL - 1,
                                    pattern=[[DL, DB], [0, DL]], channel_multiplier=-1))
            step(pool.tensor_copy(of_seq[:], v[:, :, 0]))
            step(pool.tensor_tensor(upto_s[:], same_s[:], upto[0:NS, 0:NS], ALU.mult))
            pool.tensor_scalar(cut_s[:], upto_s[:], -NEG, NEG, ALU.mult, ALU.add).then_inc(consts, 1)

            def split(u, slot):
                pool.wait_ge(w_hi, u + 1)
                pool.tensor_tensor(wlo[:, slot, :], stage[:, slot, :], whi[:, slot, :].bitcast(F32), ALU.subtract)\
                    .then_inc(w_lo, 1)

            def norm(n):
                for c in range(NC):
                    pool.wait_ge(n_hi, n * NC + c + 1)
                    pool.tensor_tensor(chunk(xlo, c), work[c % 2], chunk(xhi, c).bitcast(F32), ALU.subtract)\
                        .then_inc(n_lo, 1)

            split(0, 0)
            split(1, 1)
            norm(N_PW1)

            pool.wait_ge(n_lo, NC)
            step(pool.memset(glu[0][:, SG:SG + HIST], 0.0))
            step(pool.memset(glu[1][:, SG:SG + HIST], 0.0))
            step(pool.memset(tail, 0.0))
            pool.wait_ge(h_kept, 4)

            def history(m, a):
                wait(pool, g_conv, m - 1)
                apart(pool)
                pool.tensor_copy(glu[a][:, 0:SG].rearrange("p (b r) -> p b r", b=DB)[:, :, 0:HIST],
                                 hist[:, ds(m, 1), :].rearrange("p a (b r) -> p (a b) r", b=DB)).then_inc(g_ready, 1)
                wt = params[:, C_WDW:C_WDW + CW * KT].rearrange("p (t k) -> p t k", k=KT)
                pool.tensor_tensor(diag[a], ident[:].unsqueeze(1).to_broadcast([P, CT, P]),
                                   wt[:, CW - CT:CW, ds(m, 1)].to_broadcast([P, CT, P]), ALU.mult).then_inc(d_ready, 1)

            def tails(m, a):
                pool.wait_ge(g_glu, NC * m + NC)
                apart(pool)
                pool.tensor_copy(tail[:, ds(m, 1), 0:HIST].rearrange("p a r -> p (a r)"), glu[a][:, GW - HIST:GW])
                pool.tensor_copy(tail[:, ds(m, 1), 32:32 + NS].rearrange("p a (b r) -> p (a b) r", b=DB),
                                 glu[a][:, 0:SG].rearrange("p (b r) -> p b r", b=DB)[:, :, HIST:]).then_inc(g_tail, 1)

            history(0, 0)
            for m in range(2):
                if m == 0:
                    history(1, 1)
                split(2 * m + 2, 0)
                split(2 * m + 3, 1)
                tails(m, m)
            with pool.Fori(1, KT // 2) as m2:
                for a in range(2):
                    m = 2 * m2 + a
                    split(2 * m + 2, 0)
                    split(2 * m + 3, 1)
                    history(m, a)
                    tails(m, a)
            norm(N_LN)
            for m in range(KT):
                split(U_PW2 + 2 + m, m % 2)
            phase_end(pool, 1)

            def ffn(n, u0, nxt):
                norm(n)
                for q in range(4):
                    split(u0 + 2 + q, q % 2)
                with pool.Fori(0, FP - 1) as f:
                    for q in range(6):
                        split(u0 + 6 + 6 * f + q, q % 2)
                if nxt:
                    for q in range(2):
                        split(u0 + 6 * FP + q, q)

            ffn(N_FFN0, U_FFN0, True)
            phase_end(pool, 2)
            norm(N_SSD)
            phase_end(pool, 3)

            pool.memset(raw[:, DB * (SH + DL):DB * (SH + DL) + SH], 0.0)
            pool.memset(ctail, 0.0)
            step(pool.memset(in_seq, 1.0))
            step(pool.affine_select(out=in_seq, in_=in_seq, compare_op=ALU.is_ge, fill=0.0, base=0,
                                    pattern=[[-DL, DB], [1, NS]], channel_multiplier=0))
            step(pool.affine_select(out=in_seq, in_=in_seq, compare_op=ALU.is_ge, fill=0.0, base=DL - 1,
                                    pattern=[[DL, DB], [-1, NS]], channel_multiplier=0))

            def group(g, first):
                u = U_SSD if first else U_SSD + 8 * g - 2
                for j in range(4):
                    wait(pool, r_conv, 4 * g + j)
                    tile = (2 * g, 2 * g + 1, 2 * NG + g, 3 * NG + g)[j]
                    rsm = raw[:, 0:DB * (SH + DL)].rearrange("p (b r) -> p b r", b=DB)
                    apart(pool)
                    pool.tensor_copy(rsm[:, :, 0:SH], chist[:, ds(tile, 1), :].rearrange("p a (b r) -> p (a b) r", b=DB))\
                        .then_inc(r_ready, 1)
                    if j == 0:
                        wait(pool, ct_turned, g)
                    pool.wait_ge(r_kept, 12 * g + 3 * j + 3)
                    apart(pool)
                    pool.tensor_copy(ctail[:, j, 0:24].rearrange("p (b r) -> p b r", b=DB), rsm[:, :, DL:DL + SH])
                    pool.tensor_copy(ctail[:, j, 24:27], raw[:, RW - SH:RW]).then_inc(r_tail, 1)
                    split(u + j + 2, j % 2)
                for j in range(2):
                    split(u + j + 6, j)
                pool.wait_ge(xs_ready, 4 * g + 4)
                if not first:
                    pool.wait_ge(v_lo, 3 * g)
                pool.tensor_tensor(cmask, xs[:, 3, 0:NS].unsqueeze(1).to_broadcast([P, DB, NS]), in_seq, ALU.mult)\
                    .then_inc(masks, 1)
                pool.wait_ge(bt_ready, CH * g + 1)
                pool.tensor_tensor(bmask[0:NS], btok[0:NS].unsqueeze(1).to_broadcast([NS, DB, DS]),
                                   of_seq[:].unsqueeze(2).to_broadcast([NS, DB, DS]), ALU.mult).then_inc(masks, 1)
                xend_of(g, 0)
                for j in range(2):
                    pool.wait_ge(st_turned, 2 * g + j + 1)
                    pool.wait_ge(st_in, 32 * g + 16 * j + 16)
                    pool.wait_ge(cd_ready, g + 1)
                    pool.tensor_tensor(state_p, state_p, cdp[:, j, :].unsqueeze(2).to_broadcast([P, DB, DS]), ALU.mult)\
                        .then_inc(st_scaled, 1)
                pool.nop().then_inc(std_ready, 1)
                for c in range(1, CH):
                    xend_of(g, c)
                    pool.wait_ge(st_ready, CH * g + c)
                    pool.tensor_tensor(st_d.rearrange("p (q e) -> p q e", q=HG), st.rearrange("p (q e) -> p q e", q=HG),
                                       cendg[:, c, :].unsqueeze(2).to_broadcast([P, HG, HD]), ALU.mult).then_inc(std_ready, 1)
                    v_of(g, c - 1)
                    if not first and c == C_HALF + 1:
                        split(u + 8, 0)
                v_of(g, NCH)
                if not first:
                    split(u + 9, 1)

            def xend_of(g, c):
                n = CH * g + c
                l = NS if c == 0 else L
                pool.wait_ge(xdt_ready, n + 1)
                wait(pool, s2_done, n)
                pool.tensor_tensor(xend[0:l].rearrange("p (q e) -> p q e", q=HG), xdt[0:l].rearrange("p (q e) -> p q e", q=HG),
                                   tab[0:l, DEND, c, :].unsqueeze(2).to_broadcast([l, HG, HD]), ALU.mult).then_inc(xend_ready, 1)

            def v_of(g, c):
                n = CH * g + c
                t0, l = (0, NS) if c == 0 else (NS + (c - 1) * L, L)
                pool.wait_ge(yg_ready, n + 1)
                zs = zb[:, :, t0:t0 + l]
                pool.tensor_tensor(zs, zs, ygate.rearrange("p (j t) -> p j t", j=2)[:, :, 0:l], ALU.mult).then_inc(v_ready, 1)

            group(0, True)
            with pool.Fori(1, NG) as g:
                group(g, False)
            split(U_FFN1, 0)
            split(U_FFN1 + 1, 1)
            phase_end(pool, 4)
            ffn(N_FFN1, U_FFN1, False)
            phase_end(pool, 5)


_INS = ["x_prompt", "x_sample", "cache_conv", "state_ssd_conv", "state_ssm", "meta_tokens", "norm_mix", "norm_ffn",
        "norm_final", "cf_w_pw1", "cf_b_pw1", "cf_w_dw", "cf_b_dw", "cf_ln_g", "cf_ln_b", "cf_w_pw2", "cf_b_pw2",
        "ssd_w_in", "ssd_conv_w", "ssd_conv_b", "ssd_dt_bias", "ssd_a_log", "ssd_d", "ssd_norm_g", "ssd_w_out",
        "ffn_w_gate", "ffn_w_up", "ffn_w_down"]
_OUTS = [("y_p", (1, SEQ, D)), ("y_s", (DB, DL, D)), ("cc_p", (1, 1, HIST, D)), ("cc_s", (1, DB, HIST, D)),
         ("sc_p", (1, 1, SH, XBC)), ("sc_s", (1, DB, SH, XBC)), ("ss_p", (1, 1, NH, HD, DS)),
         ("ss_s", (1, DB, NH, HD, DS))]


def kernel(**inputs):
    import numpy as _np
    import concourse.bacc as _bacc
    from concourse.bass_utils import run_bass_kernel_spmd as _run

    nc = _bacc.Bacc("TRN2", target_bir_lowering=False, num_devices=1, dynamic_dma_scratch_size=1024)
    arrays, ins, outs = {}, {}, {}
    for name in _INS:
        a = _np.ascontiguousarray(inputs[name])
        arrays[f"in_{name}"] = a
        ins[name] = nc.dram_tensor(f"in_{name}", a.shape, mybir.dt.from_np(a.dtype), kind="ExternalInput").ap()
    for name, shape in _OUTS:
        outs[name] = nc.dram_tensor(f"out_{name}", shape, F32, kind="ExternalOutput").ap()
    hybrid_step(nc, ins, outs)
    r = _run(nc, [arrays], core_ids=[0])
    return tuple(r.results[0][f"out_{name}"] for name, _ in _OUTS)
```

```python
from contextlib import ExitStack

import concourse.bass as bass
from concourse import mybir

F32 = mybir.dt.float32
F32R = mybir.dt.float32r
BF16 = mybir.dt.bfloat16
ACT = mybir.ActivationFunctionType
ALU = mybir.AluOpType
ds = bass.ds

P = 128
D = 1024
KT = D // P
SEQ = 1024
META = 16
NP_ = META + SEQ
DB, DL = 8, 8
NS = DB * DL
T = NS + NP_
NC = 3
TC = T // NC
EPS = 1e-6
CW = 31
HIST = CW - 1
CT = 8
DI = 2 * D
NH, HD, NG, DS = 32, 64, 8, 128
HG = NH // NG
XBC = DI + 2 * NG * DS
SW = 4
SH = SW - 1
DFF = -(-8 * D // (3 * 256)) * 256
FP = DFF // 256
L = 104
NCH = NP_ // L
CH = 1 + NCH
NEG = -1e30
N_PAR_DMAS = 13
RA_SSD = 3 * KT
DT_NABS, DT_DTA, DT_END = 6, 27, 29

C_MIX, C_FFN, C_FIN, C_BPW1, C_BDW, C_LNG, C_LNB, C_BPW2, C_SNG = 0, 16, 32, 40, 56, 64, 72, 80, 88
C_WDW, C_CW, C_CB = 128, 384, 512
NPAR = 640

U_PW1 = 0
U_PW2 = U_PW1 + 2 * KT
U_FFN0 = U_PW2 + KT
U_SSD = U_FFN0 + 6 * FP
U_FFN1 = U_SSD + 8 * NG
U_END = U_FFN1 + 6 * FP
A_PW1 = 0
A_PW2 = A_PW1 + 6 * KT
A_FFN0 = A_PW2 + 3 * KT
A_SSD = A_FFN0 + 36 * FP
A_FFN1 = A_SSD + (18 + 24) * NG
N_PW1, N_LN, N_FFN0, N_SSD, N_FFN1, N_FIN = range(6)


def hybrid_step(nc, i, o):
    with ExitStack() as ctx:
        def sb(name, shape, dt=F32):
            return ctx.enter_context(nc.sbuf_tensor(name, shape, dt))

        def sem(name):
            return ctx.enter_context(nc.semaphore(name))

        h = sb("h", [P, KT, T])
        xhi = sb("xhi", [P, KT, T], F32R)
        xlo = sb("xlo", [P, KT, T], F32R)
        stage = sb("stage", [P, 2, 1024])
        whi = sb("whi", [P, 2, 1024], F32R)
        wlo = sb("wlo", [P, 2, 1024], F32R)
        ahi = sb("ahi", [P, 2, T], F32R)
        alo = sb("alo", [P, 2, T], F32R)
        ident = sb("ident", [P, P])
        identb = sb("identb", [P, P], BF16)
        mean_w = sb("mean_w", [P, P])
        upto = sb("upto", [P, L])
        upto_s = sb("upto_s", [NS, NS])
        same_s = sb("same_s", [NS, NS])
        of_seq = sb("of_seq", [NS, DB])
        cut = sb("cut", [P, L], BF16)
        cut_s = sb("cut_s", [NS, NS], BF16)
        params = sb("params", [P, NPAR])
        dvec = sb("dvec", [P, 2 * NG])
        eps = sb("eps", [P, 1])
        arena = sb("arena", [P, 18672])

        used = [0]

        def carve(n, start=None):
            if start is not None:
                used[0] = start
            a = arena[:, used[0]:used[0] + n]
            used[0] += n
            assert used[0] <= 18672, used[0]
            return a

        xrow = carve(9 * D, 0).rearrange("p (t d) -> p t d", t=9)
        prow = carve(NPAR).rearrange("p (t d) -> p t d", t=5)
        def chunk_buffer(start):
            return carve(KT * TC, start).rearrange("p (k t) -> p k t", k=KT)

        work = [chunk_buffer(0), chunk_buffer(KT * TC)]
        behind_conv = 2 * KT * TC + KT * T
        behind_ffn = 2 * KT * TC + 2 * T + 4 * TC
        work_c = work + [chunk_buffer(behind_conv)]
        work_f = work + [chunk_buffer(behind_ffn)]
        work_of = [work_c, [work_c[2], work[1], work[0]]] + [work_f] * 4
        SG = DB * (HIST + DL)
        GW = SG + HIST + NP_
        glu = [carve(GW, 0), carve(GW)]
        hist = carve(KT * DB * HIST, KT * TC).rearrange("p (k r) -> p k r", k=KT)
        tail = carve(KT * P).rearrange("p (k r) -> p k r", k=KT)
        conv = carve(KT * T, 2 * KT * TC).rearrange("p (k t) -> p k t", k=KT)
        sig = carve(NC * TC).rearrange("p (c t) -> p c t", c=NC)
        hrow = conv[:, 0:2, 0:D]
        diag = [carve(CT * P).rearrange("p (t q) -> p t q", t=CT) for a in range(2)]
        rs = [carve(TC, behind_conv + max(KT * TC, NC * TC + 2 * CT * P)), carve(TC)]
        trow = carve(D, 0)
        sg = carve(2 * T, 2 * KT * TC).rearrange("p (a t) -> p a t", a=2)
        actv = [carve(TC), carve(TC)]
        rs_f = [carve(TC), carve(TC)]
        RW = DB * (SH + DL) + SH + NP_
        raw = carve(RW, 0)
        xs = carve(4 * T).rearrange("p (j t) -> p j t", j=4)
        zb = carve(2 * T).rearrange("p (j t) -> p j t", j=2)
        state_p = carve(DB * DS).rearrange("p (b n) -> p b n", b=DB)
        state_n = carve(DB * P).rearrange("p (b q) -> p b q", b=DB)
        xdt = carve(256)
        xend = carve(256)
        dec = carve(HG * L)
        wts = carve(HG * L)
        btok = carve(DS)
        ytok = carve(256)
        yoff = carve(256)
        st = carve(256)
        st_d = carve(256)
        ygate = carve(2 * L)
        m0 = used[0]
        cmask = carve(DB * NS).rearrange("p (b l) -> p b l", b=DB)
        bmask = carve(DB * DS).rearrange("p (b n) -> p b n", b=DB)
        vsq = carve(2 * TC, m0).rearrange("p (j t) -> p j t", j=2)
        vf = carve(2 * TC).rearrange("p (j t) -> p j t", j=2)
        vrs = carve(TC, m0 + DB * NS + DB * DS)
        chist = carve(32 * 24).rearrange("p (m r) -> p m r", m=32)
        ctail = carve(P).rearrange("p (j r) -> p j r", j=4)
        ctrow = carve(P)
        stout = carve(256).rearrange("p (j n) -> p j n", j=2)
        in_seq = carve(DB * NS).rearrange("p (b l) -> p b l", b=DB)
        cdp = carve(2 * DB).rearrange("p (j b) -> p j b", j=2)
        V = CH * NH
        tabs = carve(5 * V).rearrange("p (a c h) -> p a c h", a=5, c=CH)
        DT, DTA, NACS, EACS, DEND = range(5)
        cend = carve(V).rearrange("p (c h) -> p c h", c=CH)
        tab = carve(5 * CH * HG).rearrange("p (a c h) -> p a c h", a=5, c=CH)
        cendg = carve(CH * HG).rearrange("p (c h) -> p c h", c=CH)
        q0 = behind_ffn + KT * TC
        wdt = carve(KT * P, q0).rearrange("p (k n) -> p k n", k=KT)
        dtb = carve(NH)
        alog = carve(NH)
        ev = carve(V, 2 * KT * TC)
        e1 = carve(V)
        e2 = carve(V)
        e3 = carve(V)
        dtf = carve(T)
        assert used[0] <= behind_ffn and q0 + KT * P + 2 * NH <= m0 + 1904
        crow = carve(XBC, 0)
        wdh = ahi[:, 0, 0:KT * P].rearrange("p (k n) -> p k n", k=KT)
        wdl = alo[:, 0, 0:KT * P].rearrange("p (k n) -> p k n", k=KT)
        orow = carve(9 * D, 2 * KT * TC).rearrange("p (t d) -> p t d", t=9)
        rs_o = [carve(TC), carve(TC)]

        bank = [ctx.enter_context(nc.psum_tensor(f"bank{b}", [P, 512], F32)) for b in range(8)]
        bc_bank, g_bank, t_bank, y_bank, m_bank = bank[3:8]

        w_landed = [sem("w_landed0"), sem("w_landed1")]
        w_hi, w_lo = sem("w_hi"), sem("w_lo")
        phase_done = sem("phase_done")
        acc_done = sem("acc_done")
        in_x, in_par, in_small, in_hist = sem("in_x"), sem("in_par"), sem("in_small"), sem("in_hist")
        passed = sem("passed")
        consts = sem("consts")
        cstep = sem("cstep")
        x_turned = sem("x_turned")
        x_kept = [sem("x_kept_even"), sem("x_kept_odd")]
        pstep, c_step, in_crow = sem("pstep"), sem("c_step"), sem("in_crow")
        n_sq, n_sum, n_root, n_inv, n_x, n_hi, n_lo = (sem(x) for x in (
            "n_sq", "n_sum", "n_root", "n_inv", "n_x", "n_hi", "n_lo"))
        mu_done, cen_done = sem("mu_done"), sem("cen_done")
        h_turned, h_kept = sem("h_turned"), sem("h_kept")
        g_ready, g_sig, g_glu, g_conv, g_step, g_tail = (sem(x) for x in (
            "g_ready", "g_sig", "g_glu", "g_conv", "g_step", "g_tail"))
        d_ready, tp_done, tp_kept = sem("d_ready"), sem("tp_done"), sem("tp_kept")
        tl_turned, tl_kept = sem("tl_turned"), sem("tl_kept")
        res_added = sem("res_added")
        f_gate, f_act, f_hi, f_lo, f_down = (sem(x) for x in (
            "f_gate", "f_act", "f_hi", "f_lo", "f_down"))
        stored = sem("stored")
        s_pre = sem("s_pre")
        dt_kept, dt_turned = sem("dt_kept"), sem("dt_turned")
        dt_split, dt_mm, dt_e, dt_step, dt_acs, dt_done = (sem(x) for x in (
            "dt_split", "dt_mm", "dt_e", "dt_step", "dt_acs", "dt_done"))
        ch_turned, ch_kept = sem("ch_turned"), sem("ch_kept")
        r_ready, r_kept, r_conv, r_step, r_tail = (sem(x) for x in (
            "r_ready", "r_kept", "r_conv", "r_step", "r_tail"))
        xs_ready, z_ready = sem("xs_ready"), sem("z_ready")
        ct_turned, ct_kept, ct_out = sem("ct_turned"), sem("ct_kept"), sem("ct_out")
        tab_ready = sem("tab_ready")
        st_in, st_out, sp_out = sem("st_in"), sem("st_out"), sem("sp_out")
        st_turned, st_kept, st_scaled, st_mm, st_new = (sem(x) for x in (
            "st_turned", "st_kept", "st_scaled", "st_mm", "st_new"))
        cd_mm, cd_ready, masks = sem("cd_mm"), sem("cd_ready"), sem("masks")
        s1_done, bc_done, xdt_ready, bt_ready, e_done, w_ready = (sem(x) for x in (
            "s1_done", "bc_done", "xdt_ready", "bt_ready", "e_done", "w_ready"))
        xend_ready, s2_done, yo_done, y_ready, std_ready, st_ready = (sem(x) for x in (
            "xend_ready", "s2_done", "yo_done", "y_ready", "std_ready", "st_ready"))
        s3_done, yg_ready, v_ready = sem("s3_done"), sem("yg_ready"), sem("v_ready")
        v_sq, v_sum, v_root, v_inv, v_norm, v_hi, v_lo = (sem(x) for x in (
            "v_sq", "v_sum", "v_root", "v_inv", "v_norm", "v_hi", "v_lo"))
        so_turned, so_kept = sem("so_turned"), sem("so_kept")
        o_turned = sem("o_turned")
        o_kept = [sem("o_kept_act"), sem("o_kept_dve")]

        def wait(eng, s, n):
            if not (isinstance(n, int) and n <= 0):
                eng.wait_ge(s, n)

        def apart(eng):
            eng.nop().then_inc(passed, 1)

        def phase_end(eng, n):
            eng.drain().then_inc(phase_done, 1)
            eng.wait_ge(phase_done, 4 * n)

        def chunk(t, c):
            return t[:, :, c * TC:(c + 1) * TC]

        def keep_tokens(eng, q):
            t, k0 = q // 2, 4 * (q % 2)
            n = P if t < 8 else T - 8 * P
            eng.wait_ge(x_turned, q + 1)
            dst = h[:, k0:k0 + 4, t * P:t * P + n]
            src = bank[q % 6][:, :].rearrange("p (k t) -> p k t", k=4)[:, :, 0:n]
            (eng.tensor_copy(dst, src) if q % 2 else eng.activation(dst, src, ACT.Copy)).then_inc(x_kept[q % 2], 1)

        def keep_rows(eng, q):
            t, k0 = q // 2, 4 * (q % 2)
            n = P if t < 8 else T - 8 * P
            eng.wait_ge(o_turned, q + 1)
            dst, src = orow[0:n, t, k0 * P:k0 * P + 512], bank[q % 6][0:n, :]
            if by_act(q):
                eng.activation(dst, src, ACT.Copy).then_inc(o_kept[0], 1)
            else:
                eng.tensor_copy(dst, src).then_inc(o_kept[1], 1)

        def by_act(q):
            return q < 10 or q % 2 == 0

        def rows_kept(eng, q):
            eng.wait_ge(o_kept[0 if by_act(q) else 1], sum(by_act(p) == by_act(q) for p in range(q + 1)))

        def fill(c):
            return (0 if c == 0 else 3 + 21 * (c - 1) // NCH), 3 + 21 * c // NCH

        C_HALF = next(c for c in range(CH) if fill(c)[1] >= 12)

        def parts(c):
            return (c == 0, max(c * TC - NS, 0), TC - (NS if c == 0 else 0))

        block = ctx.enter_context(nc.Block())

        @block.sync
        def _(sp):
            cm = [0]

            def weights(u, slot, view, src):
                sp.wait_ge(w_lo, u + 1)
                sp.dma_start(view, src).then_inc(w_landed[slot], 16)

            def cols(u, slot, w, n0):
                weights(u, slot, stage[:, slot, :].rearrange("p (k n) -> p k n", k=KT),
                        w.rearrange("(k p) n -> p k n", p=P)[:, :, ds(n0, P)])

            def rows(u, slot, w, pair, half):
                weights(u, slot, stage[:, slot, :].rearrange("p (k n) -> p k n", k=2),
                        w.rearrange("(k p) n -> p k n", p=P)[:, ds(2 * pair, 2), half * 512:half * 512 + 512])

            xs_src, xp = i["x_sample"].rearrange("b t d -> (b t) d"), i["x_prompt"][0]
            sp.dma_start(xrow[0:NS, 0, :], xs_src).then_inc(in_x, 16)
            sp.dma_start(xrow[NS:NS + META, 0, :], i["meta_tokens"]).then_inc(in_x, 16)
            sp.dma_start(xrow[NS + META:P, 0, :], xp[0:P - NS - META, :]).then_inc(in_x, 16)
            r0 = P - NS - META
            sp.dma_start(xrow[:, 1:8, :], xp[r0:r0 + 7 * P, :].rearrange("(t p) d -> p t d", p=P)).then_inc(in_x, 16)
            rl = SEQ - r0 - 7 * P
            sp.dma_start(xrow[0:rl, 8, :], xp[r0 + 7 * P:SEQ, :]).then_inc(in_x, 16)

            def vec(tile, row, src):
                n = src.shape[0]
                sp.dma_start(prow[row:row + n, tile, :], src).then_inc(in_par, 16)
                cm[0] += 1

            sp.wait_ge(consts, 1)
            for col, name in ((C_MIX, "norm_mix"), (C_FFN, "norm_ffn")):
                vec(0, col, i[name].rearrange("l (k d) -> (l k) d", d=P))
            for col, name in ((C_BPW1, "cf_b_pw1"), (C_BDW, "cf_b_dw"), (C_LNG, "cf_ln_g"),
                              (C_LNB, "cf_ln_b"), (C_BPW2, "cf_b_pw2"), (C_SNG, "ssd_norm_g")):
                vec(0, col, i[name][0].rearrange("(k d) -> k d", d=P))
            vec(0, C_FIN, i["norm_final"].rearrange("(k d) -> k d", d=P))
            wd = i["cf_w_dw"][0].rearrange("t (k d) -> (t k) d", d=P)
            vec(1, 0, wd[0:P, :])
            vec(2, 0, wd[P:CW * KT, :])
            vec(3, 0, i["ssd_conv_w"][0].rearrange("t (k d) -> (t k) d", d=P))
            vec(4, 0, i["ssd_conv_b"][0].rearrange("(k d) -> k d", d=P))
            assert cm[0] == N_PAR_DMAS
            for half in range(2):
                sp.dma_start(dvec[half * HD:(half + 1) * HD, :],
                             i["ssd_d"][0].rearrange("(m a) -> a m", a=2)[half:half + 1, :].broadcast_to([HD, 2 * NG]),
                             allow_slow_non_contiguous=True).then_inc(in_small, 16)
            cols(0, 0, i["cf_w_pw1"][0], 0)
            cols(1, 1, i["cf_w_pw1"][0], D)
            sp.dma_start(o["cc_s"][0][:, 0:HIST - DL, :], i["cache_conv"][0][:, DL:HIST, :]).then_inc(stored, 16)
            sp.wait_ge(x_kept[0], 9)
            sp.wait_ge(x_kept[1], 9)
            sp.dma_start(hrow[0:120, 0, :], i["cache_conv"][0].rearrange("b r d -> (b r) d")[0:120, :]).then_inc(in_hist, 16)
            sp.dma_start(hrow[0:120, 1, :], i["cache_conv"][0].rearrange("b r d -> (b r) d")[120:240, :]).then_inc(in_hist, 16)
            cols(2, 0, i["cf_w_pw1"][0], P)
            cols(3, 1, i["cf_w_pw1"][0], D + P)
            with sp.Fori(1, KT // 2) as m2:
                for a in range(2):
                    cols(4 * m2 + 2 * a, 0, i["cf_w_pw1"][0], m2 * (2 * P) + a * P)
                    cols(4 * m2 + 2 * a + 1, 1, i["cf_w_pw1"][0], m2 * (2 * P) + D + a * P)
            with sp.Fori(0, KT // 2) as m2:
                for a in range(2):
                    cols(U_PW2 + 2 * m2 + a, a, i["cf_w_pw2"][0], m2 * (2 * P) + a * P)

            def ffn(layer, u0):
                g_, u_, d_ = i["ffn_w_gate"][layer], i["ffn_w_up"][layer], i["ffn_w_down"][layer]
                for j in range(2):
                    cols(u0 + j, j, g_, j * P)
                for j in range(2):
                    cols(u0 + 2 + j, j, u_, j * P)
                with sp.Fori(0, FP - 1) as f:
                    for j in range(2):
                        cols(u0 + 4 + 6 * f + j, j, g_, f * (2 * P) + (2 + j) * P)
                    for j in range(2):
                        rows(u0 + 6 + 6 * f + j, j, d_, f, j)
                    for j in range(2):
                        cols(u0 + 8 + 6 * f + j, j, u_, f * (2 * P) + (2 + j) * P)
                for j in range(2):
                    rows(u0 + 6 * FP - 2 + j, j, d_, FP - 1, j)

            ffn(0, U_FFN0)

            w_in, w_out = i["ssd_w_in"][0], i["ssd_w_out"][0]
            cols(U_SSD, 0, w_in, DI)
            cols(U_SSD + 1, 1, w_in, DI + P)
            sp.wait_ge(n_lo, NC * 2)
            sp.dma_start(wdt, w_in.rearrange("(k p) n -> p k n", p=P)[:, :, DI + XBC + NH - P:DI + XBC + NH]).then_inc(s_pre, 16)
            sp.dma_start(dtb, i["ssd_dt_bias"].broadcast_to([P, NH])).then_inc(s_pre, 16)
            sp.dma_start(alog, i["ssd_a_log"].broadcast_to([P, NH])).then_inc(s_pre, 16)
            sp.wait_ge(n_lo, NC * 4)
            sp.wait_ge(dt_split, 1)
            sp.dma_start(crow[0:24, :], i["state_ssd_conv"][0].rearrange("b r d -> (b r) d")).then_inc(in_crow, 16)

            def group(g, first, last=False):
                u = U_SSD if first else U_SSD + 8 * g - 2
                cols(u + 2, 0, w_in, g * P + 2 * DI)
                cols(u + 3, 1, w_in, g * P + 2 * DI + NG * DS)
                cols(u + 4, 0, w_in, g * 256)
                cols(u + 5, 1, w_in, g * 256 + P)
                wait(sp, st_out, 32 * g)
                sp.wait_ge(phase_done, 4)
                s_in = i["state_ssm"][0].rearrange("b (g q) p n -> g (q p) b n", g=2 * NG)
                s_o = o["ss_s"][0].rearrange("b (g q) p n -> g (q p) b n", g=2 * NG)
                sp.dma_start(state_p, s_in[ds(2 * g, 1)].rearrange("a p b n -> (a p) b n")).then_inc(st_in, 16)
                if first:
                    cols(u + 6, 0, w_in, g * 256 + DI + 256)
                    cols(u + 7, 1, w_in, g * 256 + DI + 256 + P)
                else:
                    rows(u + 6, 0, w_out, g - 1, 0)
                    rows(u + 7, 1, w_out, g - 1, 1)
                sp.wait_ge(ct_kept, g + 1)
                for j, c0 in enumerate((g * 256, g * 256 + P, g * P + DI, g * P + DI + NG * DS)):
                    sp.dma_start(o["sc_s"][0].rearrange("b r d -> (b r) d")[:, ds(c0, P)],
                                 ctrow[32 * j:32 * j + 24, :]).then_inc(ct_out, 16)
                    sp.dma_start(o["sc_p"][0, 0][:, ds(c0, P)], ctrow[32 * j + 24:32 * j + 27, :]).then_inc(ct_out, 16)
                for j in range(2):
                    if j == 1 and last:
                        rows(u + 8, 0, w_out, g, 0)
                        rows(u + 9, 1, w_out, g, 1)
                    elif j == 1 and not first:
                        cols(u + 8, 0, w_in, g * 256 + DI + 256)
                        cols(u + 9, 1, w_in, g * 256 + DI + 256 + P)
                    sp.wait_ge(st_new, 4 * g + 2 * j + 2)
                    sp.dma_start(s_o[ds(2 * g + j, 1)].rearrange("a p b n -> (a p) b n"), state_p).then_inc(st_out, 16)
                    if j == 0:
                        sp.wait_ge(st_out, 32 * g + 16)
                        sp.dma_start(state_p, s_in[ds(2 * g + 1, 1)].rearrange("a p b n -> (a p) b n")).then_inc(st_in, 16)
                sp.wait_ge(so_kept, g + 1)
                sp.dma_start(o["ss_p"][0, 0].rearrange("(g j q) p n -> g (q p) j n", g=NG, j=2)[ds(g, 1)].rearrange("a p j n -> (a p) j n"),
                             stout).then_inc(sp_out, 16)

            group(0, True)
            with sp.Fori(1, NG - 1) as g:
                group(g, False)
            group(NG - 1, False, last=True)
            ffn(1, U_FFN1)

            yp, ys = o["y_p"][0], o["y_s"].rearrange("b t d -> (b t) d")
            rows_kept(sp, 1)
            sp.dma_start(ys, orow[0:NS, 0, :]).then_inc(stored, 16)
            sp.dma_start(yp[0:r0, :], orow[NS + META:P, 0, :]).then_inc(stored, 16)
            for t in (1, 5):
                t1 = 5 if t == 1 else 8
                rows_kept(sp, 2 * t1 - 2)
                rows_kept(sp, 2 * t1 - 1)
                sp.dma_start(yp[r0 + (t - 1) * P:r0 + (t1 - 1) * P, :].rearrange("(t p) d -> p t d", p=P),
                             orow[:, t:t1, :]).then_inc(stored, 16)
            rows_kept(sp, 16)
            rows_kept(sp, 17)
            sp.dma_start(yp[r0 + 7 * P:SEQ, :], orow[0:rl, 8, :]).then_inc(stored, 16)
            sp.wait_ge(stored, 16 * (1 + 1 + DB + 5))
            sp.wait_ge(ct_out, 16 * 8 * NG)
            sp.wait_ge(st_out, 32 * NG)
            sp.wait_ge(sp_out, 16 * NG)

        @block.tensor
        def _(pe):
            def turn(out, in_, k=P):
                return pe.transpose(out, in_, ident[0:k, 0:k])

            def dense(b, slot, offs, hi, lo, c):
                cs = slice(c * TC, (c + 1) * TC)
                n = 0
                for k, w0 in enumerate(offs):
                    for w, x in ((whi, hi), (whi, lo), (wlo, hi)):
                        mm = pe.matmul(bank[b][:, 0:TC], w[:, slot, w0:w0 + P], x[:, k, cs],
                                       start=n == 0, stop=n == 3 * len(offs) - 1)
                        n += 1
                mm.then_inc(acc_done, 1)

            FULL = [k * P for k in range(KT)]

            def unit_ready(u):
                pe.wait_ge(w_lo, u + 3)

            def norm_sums(n, cs=range(NC)):
                for c in cs:
                    q = n * NC + c
                    pe.wait_ge(n_sq, q + 1)
                    wait(pe, n_root, q - 1)
                    for k in range(KT):
                        mm = pe.matmul(bank[6 + q % 2][:, 0:TC], mean_w[:], work_of[n][c][:, k, :],
                                       start=k == 0, stop=k == KT - 1)
                    mm.then_inc(n_sum, 1)

            pe.wait_ge(consts, 2)
            pe.wait_ge(in_par, 16 * N_PAR_DMAS)
            for t in range(5):
                mm = turn(bank[6 + t // 4][:, (t % 4) * P:(t % 4 + 1) * P], prow[:, t, :])
            mm.then_inc(cstep, 1)
            pe.wait_ge(in_x, 16 * 5)
            for q in range(18):
                t, k0 = q // 2, 4 * (q % 2)
                n = P if t < 8 else T - 8 * P
                wait(pe, x_kept[q % 2], q // 2 - 2)
                for k in range(4):
                    mm = turn(bank[q % 6][:, k * P:k * P + n], xrow[0:n, t, (k0 + k) * P:(k0 + k + 1) * P], n)
                mm.then_inc(x_turned, 1)
            norm_sums(N_PW1)

            def history():
                pe.wait_ge(in_hist, 32)
                for q in range(4):
                    wait(pe, h_kept, q - 1)
                    for k in range(4):
                        mm = turn(bank[6 + q % 2][:, k * 120:(k + 1) * 120],
                                  hrow[0:120, q % 2, (4 * (q // 2) + k) * P:(4 * (q // 2) + k + 1) * P], 120)
                    mm.then_inc(h_turned, 1)

            def pair(n, u):
                for c in range(NC):
                    for v in range(2):
                        if v == 0:
                            pe.wait_ge(n_lo, n * NC + c + 1)
                        if c == 0:
                            unit_ready(u + v)
                        dense(3 * v + c, v, FULL, xhi, xlo, c)

            def pw1(m):
                for v in range(2):
                    unit_ready(U_PW1 + 2 * m + v)
                    for c in range(NC):
                        pe.wait_ge(g_glu, NC * m - 2 + c)
                        dense(3 * v + c, v, FULL, xhi, xlo, c)

            def taps(m, a, nt=CT):
                pe.wait_ge(d_ready, m + nt // CT)
                pe.wait_ge(g_glu, NC * m + NC)
                G = glu[a]
                gs = G[:, 0:SG].rearrange("p (b r) -> p b r", b=DB)
                for c in range(NC):
                    if isinstance(m, int) and m == 0:
                        pe.wait_ge(h_kept, 4)
                    wait(pe, tp_kept, NC * m + c - 1)
                    b = bank[6 + (a + c) % 2]
                    sample, t0, n = parts(c)
                    for q in range(nt):
                        t = CW - 1 - q
                        dg = diag[a ^ (q // CT)][:, CT - 1 - q % CT, :]
                        mm = pe.matmul(b[:, TC - n:TC], dg, G[:, SG + t + t0:SG + t + t0 + n],
                                       start=q == 0, stop=q == nt - 1)
                    if sample:
                        for q in range(nt):
                            t = CW - 1 - q
                            dg = diag[a ^ (q // CT)][:, CT - 1 - q % CT, :]
                            mm = pe.matmul(b[:, 0:NS], dg, gs[:, :, t:t + DL], start=q == 0, stop=q == nt - 1)
                    mm.then_inc(tp_done, 1)

            pe.wait_ge(x_kept[0], 9)
            pe.wait_ge(x_kept[1], 9)
            pair(N_PW1, U_PW1)
            history()
            pw1(1)
            taps(0, 0)
            with pe.Fori(1, KT // 2) as m2:
                pw1(2 * m2)
                taps(2 * m2 - 1, 1)
                pw1(2 * m2 + 1)
                taps(2 * m2, 0)
            taps(KT - 1, 1, 2 * CT)
            pe.wait_ge(g_tail, KT)
            pe.wait_ge(g_glu, NC * KT)
            for k in range(KT):
                mm = turn(bank[4 + k // 4][:, (k % 4) * P:(k % 4 + 1) * P], tail[:, k, :])
            mm.then_inc(tl_turned, 1)
            pe.wait_ge(g_conv, KT)
            for c in range(NC):
                wait(pe, cen_done, c - 1)
                for k in range(KT):
                    mm = pe.matmul(bank[c % 2][:, 0:TC], mean_w[:], conv[:, k, c * TC:(c + 1) * TC],
                                   start=k == 0, stop=k == KT - 1)
                mm.then_inc(mu_done, 1)
            norm_sums(N_LN)
            pe.wait_ge(tl_kept, 1)
            pe.wait_ge(cen_done, NC)

            def pw2(m, a):
                unit_ready(U_PW2 + m)
                for c in range(NC):
                    pe.wait_ge(res_added, NC * m - 5 + (2 - a) * c)
                    dense(3 * a + c, a, FULL, xhi, xlo, c)

            pair(N_LN, U_PW2)
            with pe.Fori(1, KT // 2 - 1) as m2:
                pw2(2 * m2, 0)
                pw2(2 * m2 + 1, 1)
            for c in range(NC):
                if c == NC - 1:
                    norm_sums(N_FFN0, [0])
                for a in range(2):
                    if c == 0:
                        unit_ready(U_PW2 + KT - 2 + a)
                    pe.wait_ge(res_added, NC * (KT - 4 + a) + c + 1)
                    dense(3 * a + c, a, FULL, xhi, xlo, c)
            norm_sums(N_FFN0, [1, 2])

            def ffn(n, u0, layer):
                g0, d0 = layer * 6 * FP, layer * 24 * FP

                def gate(f):
                    for j in range(2):
                        unit_ready(u0 + 6 * f - 2 + j)
                        for c in range(NC):
                            pe.wait_ge(f_act, g0 + 6 * f - 5 + 3 * j + c)
                            dense(3 * j + c, j, FULL, xhi, xlo, c)

                def up(f, first):
                    for j in range(2):
                        unit_ready(u0 + (2 + j if first else 6 * f + 2 + j))
                        for c in range(NC):
                            if first:
                                pe.wait_ge(f_gate, g0 + 2 * c + j + 1)
                            else:
                                pe.wait_ge(f_down, d0 + 24 * f - 5 + 3 * j + c)
                            dense(3 * j + c, j, FULL, xhi, xlo, c)

                def down(f, last):
                    pe.wait_ge(f_lo, g0 + 6 * f + 6)
                    for q in range(24):
                        j, m, c = (q // 4 % 2, q % 4, q // 8) if last else (q // 12, q // 3 % 4, q % 3)
                        if last and q == 16:
                            norm_sums(n + 1, [0])
                        if q == 4 * j if last else q == 12 * j:
                            unit_ready(u0 + (6 * FP - 2 + j if last else 6 * f + 6 + j))
                        if q >= 6:
                            pe.wait_ge(f_down, d0 + 24 * f + q - 5)
                        elif last:
                            pe.wait_ge(f_act, g0 + 6 * f + q + 1)
                        else:
                            pe.wait_ge(f_gate, g0 + 6 * f + 6 + q + 1)
                        dense(q % 6, j, [m * P, 512 + m * P], ahi, alo, c)

                pe.wait_ge(res_added, 3 * KT if layer == 0 else RA_SSD + 24 * NG)
                pair(n, u0)
                up(0, True)
                with pe.Fori(0, FP - 1) as f:
                    gate(f + 1)
                    down(f, False)
                    up(f + 1, False)
                down(FP - 1, True)
                norm_sums(n + 1, [1, 2])

            ffn(N_FFN0, U_FFN0, 0)

            pe.wait_ge(dt_split, 1)
            for c in range(NC):
                pe.wait_ge(n_lo, N_SSD * NC + c + 1)
                n = 0
                for k in range(KT):
                    for w, x in ((wdh, xhi), (wdh, xlo), (wdl, xhi)):
                        mm = pe.matmul(bank[c][:, 0:TC], w[:, k, :], x[:, k, c * TC:(c + 1) * TC],
                                       start=n == 0, stop=n == 3 * KT - 1)
                        n += 1
                mm.then_inc(dt_mm, 1)
            pe.wait_ge(in_crow, 16)
            for m in range(32):
                mm = turn(bank[6 + m // 16][:, (m % 16) * 24:(m % 16 + 1) * 24], crow[0:24, m * P:(m + 1) * P], 24)
            mm.then_inc(ch_turned, 1)
            pe.wait_ge(dt_kept, NC)
            for c in range(CH):
                t0 = 0 if c == 0 else NS + (c - 1) * L
                mm = turn(bank[c // 4][0:L, (c % 4) * P:(c % 4 + 1) * P], dtf[:, t0:t0 + L])
            mm.then_inc(dt_turned, 1)
            pe.wait_ge(dt_step, DT_DTA)
            pe.matmul(bank[3][0:L, NH:V], upto[0:L, :], tabs[0:L, DTA, 1:CH, :], start=True, stop=True)
            pe.matmul(bank[3][0:NS, 0:NH], upto_s[:], tabs[0:NS, DTA, 0, :], start=True, stop=True)
            pe.matmul(bank[4][:, NH:V], mean_w[0:L, :], tabs[0:L, DTA, 1:CH, :], start=True, stop=True)
            pe.matmul(bank[4][0:NS, 0:NH], same_s[:], tabs[0:NS, DTA, 0, :], start=True, stop=True).then_inc(dt_acs, 1)
            phase_end(pe, 1)

            def group(g, first, last=False):
                u = U_SSD if first else U_SSD + 8 * g - 2
                xa = A_SSD + 42 * g - (0 if first else 24)
                def proj(j, norm_before, cs=range(NC)):
                    if cs[0] == 0:
                        unit_ready(u + j)
                    for c in cs:
                        if j == 0 and not first:
                            pe.wait_ge(res_added, RA_SSD + 24 * g - 26 + c)
                            pe.wait_ge(z_ready, 6 * g)
                        elif j == 0:
                            pass
                        elif j < 4:
                            pe.wait_ge(r_kept, 12 * g + 3 * j - 2 + c)
                        elif j == 4:
                            pe.wait_ge(r_kept, 12 * g + 10 + c)
                        else:
                            pe.wait_ge(z_ready, 6 * g + c + 1)
                        dense(c, j % 2, FULL, xhi, xlo, c)
                        if j == 0 and norm_before:
                            vsum(g - 1, c)

                for j in range(4):
                    proj(j, not first)
                proj(4, False, [0, 1])
                pe.wait_ge(r_tail, 4 * g + 4)
                wait(pe, v_root, 3 * g)
                turn(m_bank[:, 0:P], ctail.rearrange("p j r -> p (j r)")).then_inc(ct_turned, 1)
                pe.wait_ge(tab_ready, g + 1)
                for q in range(HG):
                    mm = pe.matmul(m_bank[:, P + q * DB:P + (q + 1) * DB],
                                   tab[0:NS, DTA, 0, q:q + 1].to_broadcast([NS, P]), of_seq[:], start=True, stop=True)
                mm.then_inc(cd_mm, 1)

                def s1(c):
                    n = CH * g + c
                    t0, l = (0, NS) if c == 0 else (NS + (c - 1) * L, L)
                    if c == 0:
                        pe.wait_ge(xs_ready, 4 * g + 4)
                    else:
                        pe.wait_ge(w_ready, n)
                        pe.wait_ge(bt_ready, n)
                    for j in range(3):
                        turn(t_bank[0:L, j * P:(j + 1) * P], xs[:, j, t0:t0 + L])
                    pe.matmul(t_bank[0:l, 3 * P:3 * P + l], xs[:, 2, t0:t0 + l], xs[:, 3, t0:t0 + l],
                              start=True, stop=True).then_inc(s1_done, 1)
                    wait(pe, e_done, n)
                    if c == 0:
                        apart(pe)
                    ctm = (cut if c else cut_s)[0:l, 0:l].unsqueeze(1).to_broadcast([l, HG, l])
                    pe.matmul(bc_bank[0:l, 0:HG * l], identb[0:l, 0:l], ctm, start=True, stop=False)
                    for q in range(HG):
                        mm = pe.matmul(bc_bank[0:l, q * l:(q + 1) * l],
                                       tab[0:l, DTA, c, q:q + 1].to_broadcast([l, l]),
                                       (upto if c else upto_s)[0:l, 0:l], start=False, stop=q == HG - 1)
                    mm.then_inc(bc_done, 1)

                def s2(c):
                    n = CH * g + c
                    t0, l = (0, NS) if c == 0 else (NS + (c - 1) * L, L)
                    pe.wait_ge(w_ready, n + 1)
                    wait(pe, y_ready, n)
                    for q in range(HG):
                        pe.matmul(y_bank[0:l, q * HD:(q + 1) * HD], wts[0:l, q * l:(q + 1) * l],
                                  xdt[0:l, q * HD:(q + 1) * HD], start=True, stop=True)
                    pe.wait_ge(st_ready, n)
                    pe.wait_ge(bt_ready, n + 1)
                    pe.wait_ge(xend_ready, n + 1)
                    pe.matmul(y_bank[0:l, 256:512], xs[:, 3, t0:t0 + l], st, start=True, stop=True)
                    pe.matmul(m_bank[:, 0:256], btok[0:l, :], xend[0:l, :], start=True, stop=True).then_inc(s2_done, 1)

                def s3(c):
                    n = CH * g + c
                    l = NS if c == 0 else L
                    pe.wait_ge(y_ready, n + 1)
                    wait(pe, yg_ready, n)
                    if c == 0:
                        pe.wait_ge(st_new, 4 * g + 4)
                        apart(pe)
                    for j in range(2):
                        mm = turn(g_bank[:, j * L:j * L + l], ytok[0:l, j * P:(j + 1) * P], l)
                    mm.then_inc(s3_done, 1)

                def turn_states(j):
                    pe.wait_ge(st_in, 32 * g + 16 * j + 16)
                    if j == 0:
                        pe.wait_ge(e_done, CH * g + 1)
                        wait(pe, yg_ready, CH * g)
                    else:
                        pe.wait_ge(st_new, 4 * g + 2)
                    for b in range(DB):
                        mm = turn(bank[3 + b // 4][:, (b % 4) * P:(b % 4 + 1) * P], state_p[:, b, :])
                    mm.then_inc(st_turned, 1)

                def use_states(j):
                    pe.wait_ge(st_kept, 4 * g + 2 * j + 2)
                    pe.wait_ge(masks, 2 * g + 2)
                    for b in range(DB):
                        mm = pe.matmul(y_bank[0:NS, 256 + j * P:256 + (j + 1) * P], cmask[:, b, :], state_n[:, b, :],
                                       start=b == 0, stop=b == DB - 1)
                    if j == 1:
                        mm.then_inc(s2_done, 1)
                    pe.wait_ge(xend_ready, CH * g + 1)
                    for q in range(2):
                        pe.matmul(bank[7 - 3 * q][:, :], xend[0:NS, j * P:(j + 1) * P],
                                  bmask[0:NS, 4 * q:4 * q + 4, :], start=True, stop=True).then_inc(st_mm, 1)

                s1(0)
                proj(4, False, [2])
                pe.wait_ge(w_ready, CH * g + 1)
                pe.wait_ge(bt_ready, CH * g + 1)
                wait(pe, y_ready, CH * g)
                pe.wait_ge(cd_ready, g + 1)
                apart(pe)
                for q in range(HG):
                    pe.matmul(y_bank[0:NS, q * HD:(q + 1) * HD], wts[0:NS, q * NS:(q + 1) * NS],
                              xdt[0:NS, q * HD:(q + 1) * HD], start=True, stop=True)
                turn_states(0)
                proj(5, False, [0])
                use_states(0)
                proj(5, False, [1, 2])
                turn_states(1)
                if not first:
                    for k in range(fill(0)[1] - 1):
                        out_acc(g, u + 6, k, False)
                use_states(1)
                s1(1)
                s3(0)
                if not first:
                    out_acc(g, u + 6, fill(0)[1] - 1, False)
                s1(2)
                for c in range(1, CH):
                    s2(c)
                    if not first:
                        for k in range(*fill(c)):
                            out_acc(g, u + 6, k, k >= 3)
                    if c + 2 < CH:
                        s1(c + 2)
                    s3(c)
                pe.wait_ge(st_ready, CH * g + CH)
                for j in range(2):
                    mm = turn(m_bank[:, j * P:(j + 1) * P], st[:, j * P:(j + 1) * P])
                mm.then_inc(so_turned, 1)

            def out_acc(g, u, k, behind):
                j, m, c = k // 12, k // 3 % 4, k % 3
                if k % 12 == 0:
                    unit_ready(u + j)
                if behind:
                    pe.wait_ge(res_added, RA_SSD + 24 * g - 26 + k)
                elif k == 0:
                    pe.wait_ge(v_lo, 3 * g)
                    pe.wait_ge(z_ready, 6 * g + 6)
                dense(c, j, [m * P, 512 + m * P], ahi, alo, c)

            def vsum(g, c):
                pe.wait_ge(v_sq, 3 * g + c + 1)
                wait(pe, v_root, 3 * g + c)
                if c == 0:
                    pe.wait_ge(so_kept, g + 1)
                for j in range(2):
                    mm = pe.matmul(m_bank[:, 0:TC], mean_w[:], vsq[:, j, :], start=j == 0, stop=j == 1)
                mm.then_inc(v_sum, 1)

            group(0, True)
            with pe.Fori(1, NG) as g:
                group(g, False)
            phase_end(pe, 2)
            vsum(NG - 1, 0)
            for q in range(24):
                j, m, c = q // 4 % 2, q % 4, q // 8
                if q == 16:
                    norm_sums(N_FFN1, [0])
                if q % 8 == 0:
                    pe.wait_ge(v_lo, 3 * (NG - 1) + c + 1)
                    if c + 1 < NC:
                        vsum(NG - 1, c + 1)
                if q == 4 * j:
                    unit_ready(U_FFN1 - 2 + j)
                if q >= 6:
                    pe.wait_ge(res_added, RA_SSD + 24 * (NG - 1) + q - 5)
                dense(q % 6, j, [m * P, 512 + m * P], ahi, alo, c)
            norm_sums(N_FFN1, [1, 2])

            ffn(N_FFN1, U_FFN1, 1)
            for q in range(18):
                t, k0 = q // 2, 4 * (q % 2)
                n = P if t < 8 else T - 8 * P
                pe.wait_ge(n_x, N_FIN * NC + (t * P + n - 1) // TC + 1)
                if q >= 6:
                    rows_kept(pe, q - 6)
                for k in range(4):
                    mm = turn(bank[q % 6][0:n, k * P:(k + 1) * P], h[:, k0 + k, t * P:t * P + n])
                mm.then_inc(o_turned, 1)

        @block.scalar
        def _(act):
            def split(u, slot, done):
                act.wait_ge(w_landed[slot], 8 * (u - slot) + 16)
                wait(act, acc_done, done)
                act.activation(whi[:, slot, :], stage[:, slot, :], ACT.Copy).then_inc(w_hi, 1)

            def norm(n, src, affine=None, u=None):
                final = {N_LN: lambda c: (cen_done, c + 1), N_FFN0: lambda c: (res_added, 3 * KT - 6 + 2 * (c + 1)),
                         N_SSD: lambda c: (f_down, 24 * FP - 24 + 8 * (c + 1)),
                         N_FFN1: lambda c: (res_added, RA_SSD + 24 * (NG - 1) + 8 * (c + 1)),
                         N_FIN: lambda c: (f_down, 48 * FP - 24 + 8 * (c + 1))}
                rt = (rs, rs, rs_f, rs_f, rs_f, rs_o)[n]
                wk = work_of[n]

                def square(c):
                    if n in final:
                        act.wait_ge(*final[n](c))
                    if n == N_LN and c == 2:
                        act.wait_ge(stored, 16 * (2 + DB))
                    act.activation(wk[c], chunk(src, c), ACT.Square).then_inc(n_sq, 1)

                def root(c):
                    q = n * NC + c
                    act.wait_ge(n_sum, q + 1)
                    if c == 2:
                        act.wait_ge(n_x, q - 1)
                    act.activation(rt[c % 2], bank[6 + q % 2][:, 0:TC], ACT.Sqrt, bias=eps[:, 0:1]).then_inc(n_root, 1)

                def hi(c):
                    q = n * NC + c
                    act.wait_ge(n_x, q + 1)
                    if affine:
                        for k in range(KT):
                            a = act.activation(wk[c][:, k, :], conv[:, k, c * TC:(c + 1) * TC], ACT.Silu,
                                               bias=params[:, C_LNB + k:C_LNB + k + 1],
                                               scale=params[:, C_LNG + k:C_LNG + k + 1])
                        a.then_inc(g_step, 1)
                        act.wait_ge(g_step, c + 1)
                    act.activation(chunk(xhi, c), wk[c], ACT.Copy).then_inc(n_hi, 1)

                square(0)
                square(1)
                root(0)
                square(2)
                if u is not None:
                    for j in range(2):
                        split(u[0] + j, j, u[1])
                if n == N_SSD:
                    act.wait_ge(s_pre, 48)
                    act.activation(wdh, wdt, ACT.Copy).then_inc(dt_e, 1)
                root(1)
                if n != N_FIN:
                    hi(0)
                root(2)
                if n != N_FIN:
                    hi(1)
                    hi(2)

            split(0, 0, 0)
            split(1, 1, 0)
            act.wait_ge(cstep, 1)
            act.activation(params[:, 0:512], bank[6][:], ACT.Copy).then_inc(cstep, 1)
            act.activation(params[:, 512:640], bank[7][:, 0:P], ACT.Copy).then_inc(cstep, 1)
            for q in range(0, 18, 2):
                keep_tokens(act, q)
            act.wait_ge(consts, 2)
            act.wait_ge(x_kept[1], 9)
            act.wait_ge(x_kept[0], 9)
            norm(N_PW1, h)

            def gates(m, a, first):
                if first:
                    act.wait_ge(n_lo, NC)
                for c in range(NC):
                    if first and c == 2:
                        split(2 * m + 2, 0, A_PW1 + 5)
                    act.wait_ge(acc_done, A_PW1 + (2 * c + 2 if first else 6 * m + 3 + c + 1))
                    if not first:
                        act.wait_ge(g_glu, NC * m + c - 2)
                    apart(act)
                    act.activation(sig[:, c, :], bank[3 + c][:, 0:TC], ACT.Sigmoid,
                                   bias=params[:, ds(C_BPW1 + KT + m, 1)]).then_inc(g_sig, 1)
                    if not first and c == 0:
                        split(2 * m + 2, 0, A_PW1 + 6 * m + 3)
                split(2 * m + 3, 1, A_PW1 + 6 * m + 6)

            def tap_sums(m, a):
                for c in range(NC):
                    act.wait_ge(tp_done, NC * m + c + 1)
                    apart(act)
                    act.activation(conv[:, ds(m, 1), c * TC:(c + 1) * TC].rearrange("p a t -> p (a t)"),
                                   bank[6 + (a + c) % 2][:, 0:TC], ACT.Identity,
                                   bias=params[:, ds(C_BDW + m, 1)]).then_inc(tp_kept, 1)

            gates(0, 0, True)
            gates(1, 1, False)
            tap_sums(0, 0)
            with act.Fori(1, KT // 2) as m2:
                gates(2 * m2, 0, False)
                tap_sums(2 * m2 - 1, 1)
                gates(2 * m2 + 1, 1, False)
                tap_sums(2 * m2, 0)
            tap_sums(KT - 1, 1)
            act.wait_ge(tl_turned, 1)
            act.wait_ge(g_conv, KT)
            act.activation(trow[:, 0:512], bank[4][:], ACT.Copy)
            act.activation(trow[:, 512:1024], bank[5][:], ACT.Copy).then_inc(tl_kept, 1)
            act.wait_ge(tl_kept, 1)
            act.dma_start(o["cc_p"][0, 0], trow[0:HIST, :]).then_inc(stored, 16)
            for b in range(DB):
                act.dma_start(o["cc_s"][0, b, HIST - DL:HIST, :], trow[32 + b * DL:32 + (b + 1) * DL, :]).then_inc(stored, 16)
            norm(N_LN, conv, affine=True)
            for m in range(KT - 2):
                split(U_PW2 + 2 + m, m % 2, A_PW2 + (5 if m == 0 else 3 * m + 3))

            def ffn(n, u0, layer):
                norm(n, h, u=(u0, A_FFN0 if layer == 0 else A_FFN1))
                g0 = layer * 6 * FP
                a0 = A_FFN0 if layer == 0 else A_FFN1

                def gate(f, first):
                    for q in range(6):
                        j, c = (q % 2, q // 2) if first else (q // 3, q % 3)
                        act.wait_ge(acc_done, a0 + (q + 1 if first else 36 * f - 24 + q + 1))
                        if not first:
                            act.wait_ge(f_act, g0 + 6 * f)
                        act.activation(sg[:, j, c * TC:(c + 1) * TC], bank[3 * j + c][:, 0:TC], ACT.Silu)\
                           .then_inc(f_gate, 1)
                        if first and c == 2:
                            split(u0 + 2 + j, j, a0 + q + 1)
                        elif not first and c == 2:
                            split(u0 + 6 * f + j, j, a0 + 3 * j + 3 + 36 * f - 24)

                def up(f, first, last=False):
                    for j in range(2):
                        for c in range(NC):
                            q = 3 * j + c
                            act.wait_ge(f_act, g0 + 6 * f + q + 1)
                            act.activation(ahi[:, j, c * TC:(c + 1) * TC], actv[q % 2], ACT.Copy).then_inc(f_hi, 1)
                        if first:
                            split(u0 + 4 + j, j, a0 + 6 + 3 * j + 3)
                        else:
                            split(u0 + 6 * f + 4 + j, j, a0 + 36 * f + 6 + 3 * j + 3)

                gate(0, True)
                up(0, True)
                with act.Fori(0, FP - 1) as f:
                    gate(f + 1, False)
                    for j in range(2):
                        split(u0 + 6 * f + 8 + j, j, a0 + 36 * f + 18 + 12 * (j + 1))
                    up(f + 1, False)

            ffn(N_FFN0, U_FFN0, 0)

            norm(N_SSD, h, u=(U_SSD, A_SSD))
            for c in range(NC):
                act.wait_ge(dt_mm, c + 1)
                act.activation(dtf[:, c * TC:(c + 1) * TC], bank[c][:, 0:TC], ACT.Copy).then_inc(dt_kept, 1)
            act.activation(alog, alog, ACT.Exp).then_inc(dt_e, 1)
            act.wait_ge(dt_step, DT_NABS)
            act.activation(e1, e1, ACT.Exp).then_inc(dt_e, 1)
            act.wait_ge(ch_turned, 1)
            for q in range(2):
                a = act.activation(chist[:, 16 * q:16 * q + 16, :].rearrange("p m r -> p (m r)"),
                                   bank[6 + q][:, 0:16 * 24], ACT.Copy)
            a.then_inc(ch_kept, 1)
            act.wait_ge(dt_acs, 1)
            act.activation(tabs[0:L, NACS, 1:CH, :], bank[3][0:L, NH:V].rearrange("p (c h) -> p c h", h=NH), ACT.Copy, scale=-1.0)
            act.activation(tabs[0:NS, NACS, 0, :], bank[3][0:NS, 0:NH], ACT.Copy, scale=-1.0).then_inc(dt_e, 1)
            act.activation(tabs[0:L, EACS, 1:CH, :], bank[3][0:L, NH:V].rearrange("p (c h) -> p c h", h=NH), ACT.Exp)
            act.activation(tabs[0:NS, EACS, 0, :], bank[3][0:NS, 0:NH], ACT.Exp)
            act.activation(cend[:, 1:CH, :], bank[4][:, NH:V].rearrange("p (c h) -> p c h", h=NH), ACT.Exp, scale=float(D)).then_inc(dt_e, 1)
            act.wait_ge(dt_step, DT_END)
            act.activation(tabs[0:L, DEND, 1:CH, :], tabs[0:L, DEND, 1:CH, :], ACT.Exp)
            act.activation(tabs[0:NS, DEND, 0, :], tabs[0:NS, DEND, 0, :], ACT.Exp).then_inc(dt_e, 1)
            phase_end(act, 1)

            def vnorm_a(g, c):
                act.wait_ge(v_ready, CH * g + CH)
                act.activation(vsq, chunk(zb, c), ACT.Square).then_inc(v_sq, 1)

            def vnorm_b(g, c):
                act.wait_ge(v_sum, 3 * g + c + 1)
                wait(act, v_norm, 3 * g + c)
                act.activation(vrs, m_bank[:, 0:TC], ACT.Sqrt, bias=eps[:, 0:1], scale=D / 256.0).then_inc(v_root, 1)
                if c + 1 < NC:
                    vnorm_a(g, c + 1)

            def vnorm_c(g, c):
                act.wait_ge(v_norm, 3 * g + c + 1)
                act.activation(chunk(ahi, c), vf, ACT.Copy).then_inc(v_hi, 1)

            def group(g, first):
                u = U_SSD if first else U_SSD + 8 * g - 2
                xa = A_SSD if first else A_SSD + 42 * g - 24
                for j in range(4):
                    for c in range(NC):
                        if j == 0 and not first:
                            if c == 0:
                                vnorm_a(g - 1, 0)
                            vnorm_b(g - 1, c)
                        act.wait_ge(acc_done, xa + 3 * j + c + 1)
                        if c == 0:
                            act.wait_ge(r_ready, 4 * g + j + 1)
                        sample, t0, n = parts(c)
                        if sample:
                            act.activation(raw[:, 0:DB * (SH + DL)].rearrange("p (b r) -> p b r", b=DB)[:, :, SH:SH + DL],
                                           bank[c][:, 0:NS].rearrange("p (b r) -> p b r", b=DB), ACT.Copy)
                        r1 = DB * (SH + DL) + SH + t0
                        act.activation(raw[:, r1:r1 + n], bank[c][:, TC - n:TC], ACT.Copy).then_inc(r_kept, 1)
                        if j == 0 and not first:
                            vnorm_c(g - 1, c)
                    split(u + j + 2, j % 2, xa + 3 * j + 3)
                    if j > 0:
                        silu(g, j - 1)
                silu(g, 3)
                def z_acc(j, cs):
                    for c in cs:
                        act.wait_ge(acc_done, xa + 12 + 3 * j + c + 1)
                        act.activation(zb[:, j, c * TC:(c + 1) * TC], bank[c][:, 0:TC], ACT.Silu).then_inc(z_ready, 1)
                    if cs[-1] == NC - 1:
                        split(u + j + 6, j, xa + 12 + 3 * j + 3)

                def keep_states(j):
                    act.wait_ge(st_turned, 2 * g + j + 1)
                    for q in range(2):
                        act.activation(state_n[:, 4 * q:4 * q + 4, :].rearrange("p b q -> p (b q)"), bank[3 + q][:], ACT.Copy)\
                           .then_inc(st_kept, 1)

                z_acc(0, [0, 1])
                act.wait_ge(ct_turned, g + 1)
                act.wait_ge(cd_mm, g + 1)
                wait(act, ct_out, 128 * g)
                act.activation(ctrow, m_bank[:, 0:P], ACT.Copy).then_inc(ct_kept, 1)
                for a in range(2):
                    ps = slice(a * HD, (a + 1) * HD)
                    v = act.activation(cdp[ps], m_bank[ps, P:P + HG * DB].rearrange("p (j a b) -> p j a b", j=2, a=2)[:, :, a, :],
                                       ACT.Exp)
                v.then_inc(cd_ready, 1)
                chunk_a(g, 0)
                z_acc(0, [2])
                keep_states(0)
                z_acc(1, [0, 1, 2])
                keep_states(1)
                for c in range(1, CH):
                    chunk_a(g, c)
                    if not first and c == C_HALF + 1:
                        split(u + 8, 0, xa + 30)
                if not first:
                    split(u + 9, 1, xa + 42)
                act.wait_ge(so_turned, g + 1)
                wait(act, sp_out, 16 * g)
                act.activation(stout.rearrange("p j n -> p (j n)"), m_bank[:, 0:256], ACT.Copy).then_inc(so_kept, 1)

            def silu(g, j):
                act.wait_ge(r_conv, 4 * g + j + 1)
                act.activation(xs[:, j, :], xs[:, j, :], ACT.Silu).then_inc(xs_ready, 1)

            def chunk_a(g, c):
                n = CH * g + c
                l = NS if c == 0 else L
                act.wait_ge(bc_done, n + 1)
                wait(act, w_ready, n)
                for q in range(HG):
                    a = act.activation(dec[0:l, q * l:(q + 1) * l], bc_bank[0:l, q * l:(q + 1) * l], ACT.Exp,
                                       bias=tab[0:l, NACS, c, q:q + 1])
                a.then_inc(e_done, 1)
                act.wait_ge(s1_done, n + 1)
                wait(act, s2_done, n)
                if c == 1:
                    act.wait_ge(masks, 2 * g + 2)
                    act.wait_ge(st_mm, 4 * g + 4)
                act.activation(btok[0:l, :], t_bank[0:l, 256:384], ACT.Copy).then_inc(bt_ready, 1)

            group(0, True)
            with act.Fori(1, NG) as g:
                group(g, False)
            phase_end(act, 2)
            vnorm_a(NG - 1, 0)
            for c in range(NC):
                vnorm_b(NG - 1, c)
                vnorm_c(NG - 1, c)
            ffn(N_FFN1, U_FFN1, 1)
            norm(N_FIN, h)
            for q in range(18):
                if by_act(q):
                    keep_rows(act, q)

        @block.vector
        def _(dve):
            def norm(n, src, gain):
                for c in range(NC):
                    q = n * NC + c
                    if n == N_SSD and c == 1:
                        dve.wait_ge(s_pre, 48)
                        dve.wait_ge(dt_e, 1)
                        dve.tensor_tensor(wdl, wdt, wdh.bitcast(F32), ALU.subtract).then_inc(dt_split, 1)
                    r = (rs, rs, rs_f, rs_f, rs_f, rs_o)[n][c % 2]
                    dve.wait_ge(n_root, q + 1)
                    dve.reciprocal(r, r).then_inc(n_inv, 1)
                    dve.wait_ge(n_inv, q + 1)
                    for k in range(KT):
                        dst = h[:, k, c * TC:(c + 1) * TC] if n == N_FIN else work_of[n][c][:, k, :]
                        v = dve.scalar_tensor_tensor(dst, src[:, k, c * TC:(c + 1) * TC],
                                                     params[:, gain + k:gain + k + 1], r, ALU.mult, ALU.mult)
                    v.then_inc(n_x, 1)

            for q in range(1, 18, 2):
                keep_tokens(dve, q)
            dve.wait_ge(cstep, 3)
            dve.wait_ge(in_small, 32)
            norm(N_PW1, h, C_MIX)
            for q in range(4):
                dve.wait_ge(h_turned, q + 1)
                if q == 0:
                    dve.wait_ge(n_lo, NC)
                dve.tensor_copy(hist[:, 4 * (q // 2):4 * (q // 2) + 4, 120 * (q % 2):120 * (q % 2) + 120],
                                bank[6 + q % 2][:, 0:480].rearrange("p (k r) -> p k r", k=4)).then_inc(h_kept, 1)

            def glu_tile(m, a):
                G = glu[a]
                gs = G[:, 0:SG].rearrange("p (b r) -> p b r", b=DB)
                for c in range(NC):
                    dve.wait_ge(g_sig, NC * m + c + 1)
                    if c == 0:
                        dve.wait_ge(g_ready, m + 1)
                    sample, t0, n = parts(c)
                    b_a = params[:, ds(C_BPW1 + m, 1)]
                    s = sig[:, c, :]
                    if sample:
                        dve.scalar_tensor_tensor(gs[:, :, HIST:HIST + DL], bank[c][:, 0:NS].rearrange("p (b r) -> p b r", b=DB),
                                                 b_a, s[:, 0:NS].rearrange("p (b r) -> p b r", b=DB), ALU.add, ALU.mult)
                    dve.scalar_tensor_tensor(G[:, SG + HIST + t0:SG + HIST + t0 + n], bank[c][:, TC - n:TC],
                                             b_a, s[:, TC - n:TC], ALU.add, ALU.mult).then_inc(g_glu, 1)
                dve.wait_ge(g_glu, NC * m + NC)

            def conv_tile(m, a, nt=CW - CT):
                G = glu[a]
                gs = G[:, 0:SG].rearrange("p (b r) -> p b r", b=DB)
                dve.wait_ge(tp_kept, NC * m + NC)
                cs = conv[:, ds(m, 1), 0:NS].rearrange("p a (b r) -> p (a b) r", b=DB)
                cp = conv[:, ds(m, 1), NS:T].rearrange("p a t -> p (a t)")
                base = 2 * (CW - CT) * m
                for t in range(nt):
                    w = params[:, ds(C_WDW + t * KT + m, 1)]
                    if t:
                        dve.wait_ge(c_step, base + 2 * t - 1)
                    dve.scalar_tensor_tensor(cp, G[:, SG + t:SG + t + NP_], w, cp, ALU.mult, ALU.add).then_inc(c_step, 1)
                    if t:
                        dve.wait_ge(c_step, base + 2 * t)
                    dve.scalar_tensor_tensor(cs, gs[:, :, t:t + DL], w, cs, ALU.mult, ALU.add).then_inc(c_step, 1)
                dve.wait_ge(c_step, base + 2 * nt)
                dve.nop().then_inc(g_conv, 1)

            glu_tile(0, 0)
            glu_tile(1, 1)
            conv_tile(0, 0)
            with dve.Fori(1, KT // 2) as m2:
                glu_tile(2 * m2, 0)
                conv_tile(2 * m2 - 1, 1)
                glu_tile(2 * m2 + 1, 1)
                conv_tile(2 * m2, 0)
            conv_tile(KT - 1, 1, CW - 2 * CT)
            for c in range(NC):
                dve.wait_ge(mu_done, c + 1)
                dve.tensor_tensor(chunk(conv, c), chunk(conv, c),
                                  bank[c % 2][:, 0:TC].unsqueeze(1).to_broadcast([P, KT, TC]), ALU.subtract)\
                   .then_inc(cen_done, 1)
            for c in range(NC):
                q = N_LN * NC + c
                dve.wait_ge(n_root, q + 1)
                dve.reciprocal(rs[c % 2], rs[c % 2]).then_inc(n_inv, 1)
                dve.wait_ge(n_inv, q + 1)
                dve.wait_ge(n_sum, q + 1)
                dve.tensor_tensor(chunk(conv, c), chunk(conv, c),
                                  rs[c % 2].unsqueeze(1).to_broadcast([P, KT, TC]), ALU.mult).then_inc(n_x, 1)

            def res(m, a):
                for c in range(NC):
                    dve.wait_ge(acc_done, A_PW2 + NC * m + c + 1)
                    hm = h[:, ds(m, 1), c * TC:(c + 1) * TC].rearrange("p a t -> p (a t)")
                    dve.scalar_tensor_tensor(hm, bank[3 * a + c][:, 0:TC], params[:, ds(C_BPW2 + m, 1)], hm,
                                             ALU.add, ALU.add).then_inc(res_added, 1)

            def res_pair(m0):
                for c in range(NC):
                    for a in range(2):
                        m = m0 + a
                        dve.wait_ge(acc_done, A_PW2 + NC * m0 + 2 * c + a + 1)
                        hm = h[:, m, c * TC:(c + 1) * TC]
                        dve.scalar_tensor_tensor(hm, bank[3 * a + c][:, 0:TC], params[:, C_BPW2 + m:C_BPW2 + m + 1], hm,
                                                 ALU.add, ALU.add).then_inc(res_added, 1)

            res_pair(0)
            with dve.Fori(1, KT // 2 - 1) as m2:
                res(2 * m2, 0)
                res(2 * m2 + 1, 1)
            res_pair(KT - 2)

            def ffn(n, layer):
                norm(n, h, C_FFN + KT * layer)
                g0 = layer * 6 * FP
                a0 = A_FFN0 if layer == 0 else A_FFN1

                def up(f, first):
                    def lo(q):
                        j, c = q // 3, q % 3
                        dve.wait_ge(f_hi, g0 + 6 * f + q + 1)
                        cs = slice(c * TC, (c + 1) * TC)
                        dve.tensor_tensor(alo[:, j, cs], actv[q % 2], ahi[:, j, cs].bitcast(F32), ALU.subtract)\
                           .then_inc(f_lo, 1)

                    for q in range(6):
                        j, c = q // 3, q % 3
                        dve.wait_ge(acc_done, a0 + (6 + q + 1 if first else 36 * f + 6 + q + 1))
                        dve.wait_ge(f_gate, g0 + (2 * c + j + 1 if first else 6 * f + q + 1))
                        wait(dve, f_lo, g0 + 6 * f + q - 1)
                        dve.tensor_tensor(actv[q % 2], sg[:, j, c * TC:(c + 1) * TC], bank[q][:, 0:TC], ALU.mult)\
                           .then_inc(f_act, 1)
                        if q:
                            lo(q - 1)
                    lo(5)

                def down(f, last):
                    for q in range(24):
                        j, m, c = (q // 4 % 2, q % 4, q // 8) if last else (q // 12, q // 3 % 4, q % 3)
                        dve.wait_ge(acc_done, a0 + (36 * FP - 24 if last else 36 * f + 18) + q + 1)
                        hm = h[:, 4 * j + m, c * TC:(c + 1) * TC]
                        dve.tensor_tensor(hm, hm, bank[q % 6][:, 0:TC], ALU.add).then_inc(f_down, 1)

                up(0, True)
                with dve.Fori(0, FP - 1) as f:
                    down(f, False)
                    up(f + 1, False)
                down(FP - 1, True)

            ffn(N_FFN0, 0)

            norm(N_SSD, h, C_MIX + KT)
            nstep = [0]
            dve.memset(tabs, 0.0).then_inc(dt_step, 1)
            nstep[0] += 1
            dve.wait_ge(dt_step, 1)

            def step(ins):
                nstep[0] += 1
                ins.then_inc(dt_step, 1)
                dve.wait_ge(dt_step, nstep[0])

            dve.wait_ge(dt_turned, 1)
            hb = [L, CH, NH]
            e3c = lambda t: t[0:L].rearrange("p (c h) -> p c h", h=NH)
            for b in range(3):
                n = min(4, CH - 4 * b)
                step(dve.tensor_tensor(e3c(ev)[:, 4 * b:4 * b + n, :],
                                       bank[b][0:L, 0:n * P].rearrange("p (c h) -> p c h", h=P)[:, :, P - NH:P],
                                       dtb[0:L].unsqueeze(1).to_broadcast([L, n, NH]), ALU.add))
            step(dve.tensor_scalar(e1[0:L], ev[0:L], -1.0, None, ALU.mult))
            step(dve.tensor_tensor(e1[0:L], e1[0:L], ev[0:L], ALU.min))
            assert nstep[0] == DT_NABS
            dve.wait_ge(dt_e, 3)
            step(dve.tensor_scalar(e2[0:L], e1[0:L], 2.0, None, ALU.add))
            step(dve.reciprocal(e2[0:L], e2[0:L]))
            step(dve.tensor_tensor(e1[0:L], e1[0:L], e2[0:L], ALU.mult))
            step(dve.tensor_tensor(e2[0:L], e1[0:L], e1[0:L], ALU.mult))
            step(dve.tensor_scalar(e3[0:L], e2[0:L], 2.0 / 15, 2.0 / 13, ALU.mult, ALU.add))
            for k in (11, 9, 7, 5, 3, 1):
                step(dve.tensor_tensor(e3[0:L], e3[0:L], e2[0:L], ALU.mult))
                step(dve.tensor_scalar(e3[0:L], e3[0:L], 2.0 / k, None, ALU.add))
            step(dve.tensor_tensor(e3[0:L], e3[0:L], e1[0:L], ALU.mult))
            flat = lambda a: tabs[0:L, a, :, :].rearrange("p c h -> p (c h)")
            step(dve.scalar_tensor_tensor(flat(DT), ev[0:L], 0.0, e3[0:L], ALU.max, ALU.add))
            step(dve.tensor_scalar(alog, alog, -1.0, None, ALU.mult))
            step(dve.tensor_tensor(tabs[0:L, DTA, :, :], tabs[0:L, DT, :, :],
                                   alog[0:L].unsqueeze(1).to_broadcast(hb), ALU.mult))
            assert nstep[0] == DT_DTA, nstep[0]
            dve.wait_ge(dt_acs, 1)
            dve.wait_ge(dt_e, 5)
            step(dve.scalar_tensor_tensor(tabs[0:L, DEND, 1:CH, :].rearrange("p c h -> p (c h)"),
                                          bank[4][0:L, NH:V], float(D),
                                          tabs[0:L, NACS, 1:CH, :].rearrange("p c h -> p (c h)"), ALU.mult, ALU.add))
            step(dve.tensor_tensor(tabs[0:NS, DEND, 0, :], bank[4][0:NS, 0:NH], tabs[0:NS, NACS, 0, :], ALU.add))
            assert nstep[0] == DT_END
            phase_end(dve, 1)

            def vnorm(g, c):
                dve.wait_ge(v_root, 3 * g + c + 1)
                dve.reciprocal(vrs, vrs).then_inc(v_inv, 1)
                dve.wait_ge(v_inv, 3 * g + c + 1)
                wait(dve, v_lo, 3 * g + c)
                for j in range(2):
                    v = dve.scalar_tensor_tensor(vf[:, j, :], zb[:, j, c * TC:(c + 1) * TC],
                                                 params[:, ds(C_SNG + 2 * g + j, 1)], vrs, ALU.mult, ALU.mult)
                v.then_inc(v_norm, 1)
                dve.wait_ge(v_hi, 3 * g + c + 1)
                dve.tensor_tensor(chunk(alo, c), vf, chunk(ahi, c).bitcast(F32), ALU.subtract).then_inc(v_lo, 1)

            def group(g, first):
                if not first:
                    dve.wait_ge(e_done, CH * g)
                    dve.wait_ge(s2_done, CH * g)
                    dve.wait_ge(s3_done, CH * g)
                    dve.wait_ge(v_ready, CH * g)
                    dve.wait_ge(std_ready, CH * g)
                    dve.wait_ge(xend_ready, CH * g)
                dve.tensor_copy(tab[0:L, :, 1:CH, :], tabs[0:L, :, 1:CH, ds(HG * g, HG)])
                dve.tensor_copy(tab[0:NS, :, 0, :], tabs[0:NS, :, 0, ds(HG * g, HG)])
                dve.tensor_copy(cendg[:, 1:CH, :], cend[:, 1:CH, ds(HG * g, HG)]).then_inc(tab_ready, 1)
                if not first:
                    for c in range(NC):
                        vnorm(g - 1, c)
                for j in range(4):
                    dve.wait_ge(r_kept, 12 * g + 3 * j + 3)
                    if j == 0:
                        wait(dve, s3_done, CH * g)
                    tile = (2 * g, 2 * g + 1, 2 * NG + g, 3 * NG + g)[j]
                    rsm = raw[:, 0:DB * (SH + DL)].rearrange("p (b r) -> p b r", b=DB)
                    rp = raw[:, DB * (SH + DL):RW]
                    os_ = xs[:, j, 0:NS].rearrange("p (b r) -> p b r", b=DB)
                    op = xs[:, j, NS:T]
                    for t in range(SW):
                        w = params[:, ds(C_CW + 32 * t + tile, 1)]
                        base = 8 * (4 * g + j)
                        if t == 0:
                            b = params[:, ds(C_CB + tile, 1)]
                            dve.tensor_scalar(op, rp[:, 0:NP_], w, b, ALU.mult, ALU.add).then_inc(r_step, 1)
                            dve.tensor_scalar(os_, rsm[:, :, 0:DL], w, b, ALU.mult, ALU.add).then_inc(r_step, 1)
                        else:
                            dve.wait_ge(r_step, base + 2 * t - 1)
                            dve.scalar_tensor_tensor(op, rp[:, t:t + NP_], w, op, ALU.mult, ALU.add).then_inc(r_step, 1)
                            dve.wait_ge(r_step, base + 2 * t)
                            dve.scalar_tensor_tensor(os_, rsm[:, :, t:t + DL], w, os_, ALU.mult, ALU.add).then_inc(r_step, 1)
                    dve.wait_ge(r_step, base + 8)
                    dve.nop().then_inc(r_conv, 1)
                chunk_in(g, 0)
                for j in range(2):
                    for q in range(2):
                        dve.wait_ge(st_mm, 4 * g + 2 * j + q + 1)
                        dve.wait_ge(st_scaled, 2 * g + j + 1)
                        sl = state_p[:, 4 * q:4 * q + 4, :].rearrange("p b n -> p (b n)")
                        dve.tensor_tensor(sl, sl, bank[7 - 3 * q][:], ALU.add).then_inc(st_new, 1)
                chunk_y(g, 0)
                wait(dve, so_turned, g)
                dve.memset(st, 0.0).then_inc(st_ready, 1)
                chunk_in(g, 1)
                for c in range(CH):
                    if c:
                        chunk_st(g, c)
                        if c + 1 < CH:
                            chunk_in(g, c + 1)
                        chunk_y(g, c)
                    else:
                        gate(g, 0)
                    if not first:
                        for k in range(*fill(c)):
                            out_res(g, k)
                    if c:
                        gate(g, c)

            def out_last(c):
                for q in range(8 * c, 8 * c + 8):
                    dve.wait_ge(acc_done, A_FFN1 - 24 + q + 1)
                    hm = h[:, q % 8, c * TC:(c + 1) * TC]
                    dve.tensor_tensor(hm, hm, bank[q % 6][:, 0:TC], ALU.add).then_inc(res_added, 1)

            def out_res(g, k):
                j, m, c = k // 12, k // 3 % 4, k % 3
                dve.wait_ge(acc_done, A_SSD + 42 * g - 6 + k + 1)
                hm = h[:, 4 * j + m, c * TC:(c + 1) * TC]
                dve.tensor_tensor(hm, hm, bank[c][:, 0:TC], ALU.add).then_inc(res_added, 1)

            def chunk_in(g, c):
                n = CH * g + c
                l = NS if c == 0 else L
                dve.wait_ge(s1_done, n + 1)
                wait(dve, s2_done, n)
                wait(dve, xend_ready, n)
                dve.wait_ge(bt_ready, n + 1)
                if c == 1:
                    dve.wait_ge(st_mm, 4 * g + 4)
                dve.tensor_tensor(xdt[0:l].rearrange("p (q e) -> p q e", q=HG),
                                  t_bank[0:l, 0:256].rearrange("p (q e) -> p q e", q=HG),
                                  tab[0:l, DT, c, :].unsqueeze(2).to_broadcast([l, HG, HD]), ALU.mult).then_inc(xdt_ready, 1)
                dve.wait_ge(e_done, n + 1)
                dve.tensor_tensor(wts[0:l, 0:HG * l].rearrange("p (q e) -> p q e", q=HG),
                                  dec[0:l, 0:HG * l].rearrange("p (q e) -> p q e", q=HG),
                                  t_bank[0:l, 384:384 + l].unsqueeze(1).to_broadcast([l, HG, l]), ALU.mult)\
                   .then_inc(w_ready, 1)

            def chunk_st(g, c):
                n = CH * g + c
                dve.wait_ge(s2_done, n + 1)
                dve.wait_ge(std_ready, n + 1)
                dve.tensor_tensor(st, st_d, m_bank[:, 0:256], ALU.add).then_inc(st_ready, 1)

            def chunk_y(g, c):
                n = CH * g + c
                l = NS if c == 0 else L
                dve.wait_ge(s2_done, n + 1)
                wait(dve, s3_done, n)
                dve.tensor_tensor(yoff[0:l].rearrange("p (q e) -> p q e", q=HG),
                                  y_bank[0:l, 256:512].rearrange("p (q e) -> p q e", q=HG),
                                  tab[0:l, EACS, c, :].unsqueeze(2).to_broadcast([l, HG, HD]), ALU.mult).then_inc(yo_done, 1)
                dve.wait_ge(yo_done, n + 1)
                dve.tensor_tensor(ytok[0:l], yoff[0:l], y_bank[0:l, 0:256], ALU.add).then_inc(y_ready, 1)

            def gate(g, c):
                n = CH * g + c
                t0, l = (0, NS) if c == 0 else (NS + (c - 1) * L, L)
                dve.wait_ge(s3_done, n + 1)
                wait(dve, v_ready, n)
                for j in range(2):
                    v = dve.scalar_tensor_tensor(ygate[:, j * L:j * L + l], xs[:, j, t0:t0 + l],
                                                 dvec[:, ds(2 * g + j, 1)], g_bank[:, j * L:j * L + l],
                                                 ALU.mult, ALU.add)
                v.then_inc(yg_ready, 1)

            group(0, True)
            with dve.Fori(1, NG) as g:
                group(g, False)
            phase_end(dve, 2)
            for c in range(NC):
                vnorm(NG - 1, c)
                if c:
                    out_last(c - 1)
            out_last(NC - 1)
            ffn(N_FFN1, 1)
            norm(N_FIN, h, C_FIN)
            for q in range(18):
                if not by_act(q):
                    keep_rows(dve, q)

        @block.gpsimd
        def _(pool):
            pool.nop().then_inc(w_lo, 2)
            n_c = [0]

            def step(ins):
                ins.then_inc(pstep, 1)
                n_c[0] += 1
                pool.wait_ge(pstep, n_c[0])

            pool.memset(prow, 0.0).then_inc(consts, 1)
            pool.memset(eps[:], EPS)
            pool.memset(mean_w[:], 1.0 / D)
            step(pool.memset(ident[:], 0.0))
            step(pool.affine_select(out=ident[:], in_=ident[:], compare_op=ALU.not_equal, fill=1.0, base=0,
                                    pattern=[[-1, P]], channel_multiplier=1))
            step(pool.tensor_copy(identb[:], ident[:]))
            step(pool.memset(upto[:], 1.0))
            step(pool.affine_select(out=upto[:], in_=upto[:], compare_op=ALU.is_ge, fill=0.0, base=0,
                                    pattern=[[1, L]], channel_multiplier=-1))
            step(pool.memset(cut[:], 0.0))
            step(pool.affine_select(out=cut[:], in_=cut[:], compare_op=ALU.is_ge, fill=NEG, base=0,
                                    pattern=[[1, L]], channel_multiplier=-1))
            v = same_s[:].rearrange("p (b r) -> p b r", b=DB)
            step(pool.memset(same_s[:], 1.0))
            step(pool.affine_select(out=v, in_=v, compare_op=ALU.is_ge, fill=0.0, base=0,
                                    pattern=[[-DL, DB], [0, DL]], channel_multiplier=1))
            step(pool.affine_select(out=v, in_=v, compare_op=ALU.is_ge, fill=0.0, base=DL - 1,
                                    pattern=[[DL, DB], [0, DL]], channel_multiplier=-1))
            step(pool.tensor_copy(of_seq[:], v[:, :, 0]))
            step(pool.tensor_tensor(upto_s[:], same_s[:], upto[0:NS, 0:NS], ALU.mult))
            pool.tensor_scalar(cut_s[:], upto_s[:], -NEG, NEG, ALU.mult, ALU.add).then_inc(consts, 1)

            def split(u, slot):
                pool.wait_ge(w_hi, u + 1)
                pool.tensor_tensor(wlo[:, slot, :], stage[:, slot, :], whi[:, slot, :].bitcast(F32), ALU.subtract)\
                    .then_inc(w_lo, 1)

            def norm(n, u=None):
                for c in range(NC):
                    if c == 0 and u is not None:
                        for j in range(2):
                            split(u + j, j)
                    pool.wait_ge(n_hi, n * NC + c + 1)
                    pool.tensor_tensor(chunk(xlo, c), work_of[n][c], chunk(xhi, c).bitcast(F32), ALU.subtract)\
                        .then_inc(n_lo, 1)

            split(0, 0)
            split(1, 1)
            norm(N_PW1)

            split(2, 0)
            split(3, 1)
            pool.wait_ge(n_lo, NC)
            step(pool.memset(glu[0][:, SG:SG + HIST], 0.0))
            step(pool.memset(glu[1][:, SG:SG + HIST], 0.0))
            step(pool.memset(tail, 0.0))
            pool.wait_ge(h_kept, 4)

            def diagonals(m, a, t):
                wt = params[:, C_WDW:C_WDW + CW * KT].rearrange("p (t k) -> p t k", k=KT)
                pool.tensor_tensor(diag[a], ident[:].unsqueeze(1).to_broadcast([P, CT, P]),
                                   wt[:, t:t + CT, ds(m, 1)].to_broadcast([P, CT, P]), ALU.mult).then_inc(d_ready, 1)

            def history(m, a):
                wait(pool, g_conv, m - 1)
                apart(pool)
                pool.tensor_copy(glu[a][:, 0:SG].rearrange("p (b r) -> p b r", b=DB)[:, :, 0:HIST],
                                 hist[:, ds(m, 1), :].rearrange("p a (b r) -> p (a b) r", b=DB)).then_inc(g_ready, 1)
                diagonals(m, a, CW - CT)

            def tails(m, a):
                pool.wait_ge(g_glu, NC * m + NC)
                apart(pool)
                pool.tensor_copy(tail[:, ds(m, 1), 0:HIST].rearrange("p a r -> p (a r)"), glu[a][:, GW - HIST:GW])
                pool.tensor_copy(tail[:, ds(m, 1), 32:32 + NS].rearrange("p a (b r) -> p (a b) r", b=DB),
                                 glu[a][:, 0:SG].rearrange("p (b r) -> p b r", b=DB)[:, :, HIST:]).then_inc(g_tail, 1)

            history(0, 0)
            for m in range(2):
                if m == 0:
                    history(1, 1)
                else:
                    split(2 * m + 2, 0)
                    split(2 * m + 3, 1)
                tails(m, m)
            with pool.Fori(1, KT // 2) as m2:
                for a in range(2):
                    m = 2 * m2 + a
                    split(2 * m + 2, 0)
                    split(2 * m + 3, 1)
                    history(m, a)
                    tails(m, a)
            pool.wait_ge(tp_done, NC * (KT - 1))
            diagonals(KT - 1, 0, CW - 2 * CT)
            norm(N_LN)
            for m in range(KT - 2):
                split(U_PW2 + 2 + m, m % 2)

            def ffn(n, u0):
                norm(n, u0)
                for q in range(4):
                    split(u0 + 2 + q, q % 2)
                with pool.Fori(0, FP - 1) as f:
                    for q in range(6):
                        split(u0 + 6 + 6 * f + q, q % 2)

            ffn(N_FFN0, U_FFN0)
            norm(N_SSD, U_SSD)
            phase_end(pool, 1)

            pool.memset(raw[:, DB * (SH + DL):DB * (SH + DL) + SH], 0.0)
            pool.memset(ctail, 0.0)
            step(pool.memset(in_seq, 1.0))
            step(pool.affine_select(out=in_seq, in_=in_seq, compare_op=ALU.is_ge, fill=0.0, base=0,
                                    pattern=[[-DL, DB], [1, NS]], channel_multiplier=0))
            step(pool.affine_select(out=in_seq, in_=in_seq, compare_op=ALU.is_ge, fill=0.0, base=DL - 1,
                                    pattern=[[DL, DB], [-1, NS]], channel_multiplier=0))

            def group(g, first):
                u = U_SSD if first else U_SSD + 8 * g - 2
                for j in range(4):
                    wait(pool, r_conv, 4 * g + j)
                    tile = (2 * g, 2 * g + 1, 2 * NG + g, 3 * NG + g)[j]
                    rsm = raw[:, 0:DB * (SH + DL)].rearrange("p (b r) -> p b r", b=DB)
                    apart(pool)
                    pool.tensor_copy(rsm[:, :, 0:SH], chist[:, ds(tile, 1), :].rearrange("p a (b r) -> p (a b) r", b=DB))\
                        .then_inc(r_ready, 1)
                    if j == 0:
                        wait(pool, ct_turned, g)
                    pool.wait_ge(r_kept, 12 * g + 3 * j + 3)
                    apart(pool)
                    pool.tensor_copy(ctail[:, j, 0:24].rearrange("p (b r) -> p b r", b=DB), rsm[:, :, DL:DL + SH])
                    pool.tensor_copy(ctail[:, j, 24:27], raw[:, RW - SH:RW]).then_inc(r_tail, 1)
                    split(u + j + 2, j % 2)
                pool.wait_ge(xs_ready, 4 * g + 4)
                if not first:
                    pool.wait_ge(v_lo, 3 * g)
                pool.tensor_tensor(cmask, xs[:, 3, 0:NS].unsqueeze(1).to_broadcast([P, DB, NS]), in_seq, ALU.mult)\
                    .then_inc(masks, 1)
                pool.wait_ge(bt_ready, CH * g + 1)
                pool.tensor_tensor(bmask[0:NS], btok[0:NS].unsqueeze(1).to_broadcast([NS, DB, DS]),
                                   of_seq[:].unsqueeze(2).to_broadcast([NS, DB, DS]), ALU.mult).then_inc(masks, 1)
                xend_of(g, 0)
                for j in range(2):
                    split(u + j + 6, j)
                    pool.wait_ge(st_turned, 2 * g + j + 1)
                    pool.wait_ge(st_in, 32 * g + 16 * j + 16)
                    pool.wait_ge(cd_ready, g + 1)
                    pool.tensor_tensor(state_p, state_p, cdp[:, j, :].unsqueeze(2).to_broadcast([P, DB, DS]), ALU.mult)\
                        .then_inc(st_scaled, 1)
                pool.nop().then_inc(std_ready, 1)
                for c in range(1, CH):
                    xend_of(g, c)
                    pool.wait_ge(st_ready, CH * g + c)
                    pool.tensor_tensor(st_d.rearrange("p (q e) -> p q e", q=HG), st.rearrange("p (q e) -> p q e", q=HG),
                                       cendg[:, c, :].unsqueeze(2).to_broadcast([P, HG, HD]), ALU.mult).then_inc(std_ready, 1)
                    v_of(g, c - 1)
                    if not first and c == C_HALF + 1:
                        split(u + 8, 0)
                v_of(g, NCH)
                if not first:
                    split(u + 9, 1)

            def xend_of(g, c):
                n = CH * g + c
                l = NS if c == 0 else L
                pool.wait_ge(xdt_ready, n + 1)
                wait(pool, s2_done, n)
                pool.tensor_tensor(xend[0:l].rearrange("p (q e) -> p q e", q=HG), xdt[0:l].rearrange("p (q e) -> p q e", q=HG),
                                   tab[0:l, DEND, c, :].unsqueeze(2).to_broadcast([l, HG, HD]), ALU.mult).then_inc(xend_ready, 1)

            def v_of(g, c):
                n = CH * g + c
                t0, l = (0, NS) if c == 0 else (NS + (c - 1) * L, L)
                pool.wait_ge(yg_ready, n + 1)
                zs = zb[:, :, t0:t0 + l]
                pool.tensor_tensor(zs, zs, ygate.rearrange("p (j t) -> p j t", j=2)[:, :, 0:l], ALU.mult).then_inc(v_ready, 1)

            group(0, True)
            with pool.Fori(1, NG) as g:
                group(g, False)
            phase_end(pool, 2)
            ffn(N_FFN1, U_FFN1)


_INS = ["x_prompt", "x_sample", "cache_conv", "state_ssd_conv", "state_ssm", "meta_tokens", "norm_mix", "norm_ffn",
        "norm_final", "cf_w_pw1", "cf_b_pw1", "cf_w_dw", "cf_b_dw", "cf_ln_g", "cf_ln_b", "cf_w_pw2", "cf_b_pw2",
        "ssd_w_in", "ssd_conv_w", "ssd_conv_b", "ssd_dt_bias", "ssd_a_log", "ssd_d", "ssd_norm_g", "ssd_w_out",
        "ffn_w_gate", "ffn_w_up", "ffn_w_down"]
_OUTS = [("y_p", (1, SEQ, D)), ("y_s", (DB, DL, D)), ("cc_p", (1, 1, HIST, D)), ("cc_s", (1, DB, HIST, D)),
         ("sc_p", (1, 1, SH, XBC)), ("sc_s", (1, DB, SH, XBC)), ("ss_p", (1, 1, NH, HD, DS)),
         ("ss_s", (1, DB, NH, HD, DS))]


def kernel(**inputs):
    import numpy as _np
    import concourse.bacc as _bacc
    from concourse.bass_utils import run_bass_kernel_spmd as _run

    nc = _bacc.Bacc("TRN2", target_bir_lowering=False, num_devices=1, dynamic_dma_scratch_size=1024)
    arrays, ins, outs = {}, {}, {}
    for name in _INS:
        a = _np.ascontiguousarray(inputs[name])
        arrays[f"in_{name}"] = a
        ins[name] = nc.dram_tensor(f"in_{name}", a.shape, mybir.dt.from_np(a.dtype), kind="ExternalInput").ap()
    for name, shape in _OUTS:
        outs[name] = nc.dram_tensor(f"out_{name}", shape, F32, kind="ExternalOutput").ap()
    hybrid_step(nc, ins, outs)
    r = _run(nc, [arrays], core_ids=[0])
    return tuple(r.results[0][f"out_{name}"] for name, _ in _OUTS)
```
